# Optimizing a Trainium2 kernel written in Bass

```python
import math
import jax, jax.numpy as jnp
from jax import lax
import numpy as np

D_MODEL = 1024
BATCH = 1
SEQ = 128
DEPTH = 2
DEC_BATCH = 1
DEC_SEQ = 1024
PAST_LEN = 128

GRID_W = 64
N_HEADS = 8
HEAD_DIM = 64
V_DIM = 2 * HEAD_DIM
ATTN_WIDTH = N_HEADS * V_DIM
ROPE_BASE = 10000.0
Q_BLOCK = 128
N_POOL_GROUPS = 4
POOL_GROUP = D_MODEL // N_POOL_GROUPS
POOL_WINDOWS = (2, 4, 8, 16)
N_EXPERTS = 16
EC_CAPACITY = 2
EXPERT_FF = 1408
N_ATTN_LAYERS = (DEPTH + 1) // 2
N_POOL_LAYERS = DEPTH // 2
EPS = 1e-6

kernel_name = 'hybrid_diffattn_pool_ec_diffusion_step'

def rmsnorm(x, g):
    xf = x.astype(jnp.float32)
    y = xf * lax.rsqrt(jnp.mean(xf * xf, axis=-1, keepdims=True) + EPS)
    return y.astype(x.dtype) * g

def modulation(cvec, w, b):
    m = jax.nn.silu(cvec) @ w + b
    return jnp.split(m, 6, axis=-1)

def adaln(x, g, shift, scale):
    return rmsnorm(x, g) * (1 + scale) + shift

def axial_rope_tables(n_tokens):
    rows = n_tokens // GRID_W
    t = jnp.arange(rows * GRID_W)
    row = (t // GRID_W).astype(jnp.float32)
    col = (t % GRID_W).astype(jnp.float32)
    half = HEAD_DIM // 2
    inv = ROPE_BASE ** (-jnp.arange(0, half, 2, dtype=jnp.float32) / half)
    ang = jnp.concatenate([row[:, None] * inv, col[:, None] * inv], axis=-1)
    return jnp.cos(ang), jnp.sin(ang)

def apply_axial_rope(x, cos, sin):
    q = HEAD_DIM // 4
    cos = cos.astype(x.dtype)[None, :, None, None, :]
    sin = sin.astype(x.dtype)[None, :, None, None, :]
    cr, cc = cos[..., :q], cos[..., q:]
    sr, sc = sin[..., :q], sin[..., q:]
    xr1, xr2 = x[..., :q], x[..., q:2 * q]
    xc1, xc2 = x[..., 2 * q:3 * q], x[..., 3 * q:]
    return jnp.concatenate([xr1 * cr - xr2 * sr, xr1 * sr + xr2 * cr,
                            xc1 * cc - xc2 * sc, xc1 * sc + xc2 * cc], axis=-1)

def project_qkv(h, w):
    b, n, _ = h.shape
    q, k, v = jnp.split(h @ w, 3, axis=-1)
    return (q.reshape(b, n, N_HEADS, 2, HEAD_DIM),
            k.reshape(b, n, N_HEADS, 2, HEAD_DIM),
            v.reshape(b, n, N_HEADS, V_DIM))

def diff_lambda(lq1, lk1, lq2, lk2, lam_init):
    return (jnp.exp(jnp.sum(lq1 * lk1).astype(jnp.float32))
            - jnp.exp(jnp.sum(lq2 * lk2).astype(jnp.float32)) + lam_init)

def diff_attention(q, k, v, lam):
    b, n, h, _, d = q.shape
    nb = n // Q_BLOCK
    qb = (q * (d ** -0.5)).reshape(b, nb, Q_BLOCK, h, 2, d).transpose(1, 0, 2, 3, 4, 5)

    def block(qi):
        s = jnp.einsum('bqhcd,bkhcd->bhcqk', qi, k).astype(jnp.float32)
        p = jax.nn.softmax(s, axis=-1)
        a = p[:, :, 0] - lam * p[:, :, 1]
        return jnp.einsum('bhqk,bkhe->bqhe', a.astype(v.dtype), v)

    o = lax.map(block, qb)
    return o.transpose(1, 0, 2, 3, 4).reshape(b, n, h, V_DIM)

def attn_output(o, g, wo, lam_init):
    b, n = o.shape[:2]
    o = rmsnorm(o, g) * (1.0 - lam_init)
    return o.reshape(b, n, ATTN_WIDTH) @ wo

def multiscale_pool(h, w, bias, scale):
    b, n, _ = h.shape
    hg = h.reshape(b, n, N_POOL_GROUPS, POOL_GROUP)
    t = jnp.arange(n)
    outs = []
    for gi, win in enumerate(POOL_WINDOWS):
        xg = hg[:, :, gi].astype(jnp.float32)
        cs = jnp.concatenate([jnp.zeros((b, 1, POOL_GROUP), jnp.float32),
                              jnp.cumsum(xg, axis=1)], axis=1)
        lo = jnp.clip(t - win // 2, 0, n)
        hi = jnp.clip(t + win // 2, 0, n)
        cnt = (hi - lo).astype(jnp.float32)[None, :, None]
        outs.append((cs[:, hi] - cs[:, lo]) / cnt - xg)
    pooled = jnp.stack(outs, axis=2).astype(h.dtype)
    y = jnp.einsum('bngc,gcd->bngd', pooled, w) + bias
    return y.reshape(b, n, D_MODEL) * scale

def expert_choice_ffn(h, w_router, w_gate, w_up, w_down):
    n, d = h.shape
    cap = EC_CAPACITY * n // N_EXPERTS
    aff = jax.nn.softmax((h @ w_router).astype(jnp.float32), axis=-1)
    g, idx = lax.top_k(aff.T, cap)
    xe = h[idx]
    hid = jax.nn.silu(jnp.einsum('ecd,edf->ecf', xe, w_gate)) * jnp.einsum('ecd,edf->ecf', xe, w_up)
    ye = jnp.einsum('ecf,efd->ecd', hid, w_down) * g[..., None].astype(h.dtype)
    return jnp.zeros_like(h).at[idx.reshape(-1)].add(ye.reshape(-1, d))

def setup_inputs(seed: int = 0) -> dict:
    key = jax.random.key(seed)
    ks = jax.random.split(key, 25)

    def nrm(k, shape, scale=1.0):
        return jax.random.normal(k, shape, jnp.float32) * scale

    return {
        'x_prompt': nrm(ks[0], (BATCH, SEQ, D_MODEL)),
        'x_sample': nrm(ks[1], (DEC_BATCH, DEC_SEQ, D_MODEL)),
        'cache_k': nrm(ks[2], (DEC_BATCH, N_ATTN_LAYERS, PAST_LEN, N_HEADS, 2 * HEAD_DIM)),
        'cache_v': nrm(ks[3], (DEC_BATCH, N_ATTN_LAYERS, PAST_LEN, N_HEADS, V_DIM)),
        'c': nrm(ks[4], (DEC_BATCH, D_MODEL)),
        'c_ctx': nrm(ks[5], (D_MODEL,)),
        'w_mod': nrm(ks[6], (DEPTH, D_MODEL, 6 * D_MODEL), 0.5 * D_MODEL ** -0.5),
        'b_mod': nrm(ks[7], (DEPTH, 6 * D_MODEL), 0.01),
        'norm1_g': 1.0 + nrm(ks[8], (DEPTH, D_MODEL), 0.02),
        'norm2_g': 1.0 + nrm(ks[9], (DEPTH, D_MODEL), 0.02),
        'attn_wqkv': nrm(ks[10], (N_ATTN_LAYERS, D_MODEL, 3 * ATTN_WIDTH), D_MODEL ** -0.5),
        'attn_wo': nrm(ks[11], (N_ATTN_LAYERS, ATTN_WIDTH, D_MODEL), ATTN_WIDTH ** -0.5),
        'lambda_q1': nrm(ks[12], (N_ATTN_LAYERS, HEAD_DIM), 0.1),
        'lambda_k1': nrm(ks[13], (N_ATTN_LAYERS, HEAD_DIM), 0.1),
        'lambda_q2': nrm(ks[14], (N_ATTN_LAYERS, HEAD_DIM), 0.1),
        'lambda_k2': nrm(ks[15], (N_ATTN_LAYERS, HEAD_DIM), 0.1),
        'subln_g': 1.0 + nrm(ks[16], (N_ATTN_LAYERS, V_DIM), 0.02),
        'pool_w': nrm(ks[17], (N_POOL_LAYERS, N_POOL_GROUPS, POOL_GROUP, POOL_GROUP), POOL_GROUP ** -0.5),
        'pool_b': nrm(ks[18], (N_POOL_LAYERS, N_POOL_GROUPS, POOL_GROUP), 0.01),
        'pool_scale': 1.0 + nrm(ks[19], (N_POOL_LAYERS, D_MODEL), 0.02),
        'router_w': nrm(ks[20], (DEPTH, D_MODEL, N_EXPERTS), D_MODEL ** -0.5),
        'expert_w_gate': nrm(ks[21], (DEPTH, N_EXPERTS, D_MODEL, EXPERT_FF), D_MODEL ** -0.5),
        'expert_w_up': nrm(ks[22], (DEPTH, N_EXPERTS, D_MODEL, EXPERT_FF), D_MODEL ** -0.5),
        'expert_w_down': nrm(ks[23], (DEPTH, N_EXPERTS, EXPERT_FF, D_MODEL), EXPERT_FF ** -0.5),
        'final_g': 1.0 + nrm(ks[24], (D_MODEL,), 0.02),
    }

def reference(x_prompt, x_sample, cache_k, cache_v, c, c_ctx, w_mod, b_mod, norm1_g, norm2_g,
              attn_wqkv, attn_wo, lambda_q1, lambda_k1, lambda_q2, lambda_k2, subln_g,
              pool_w, pool_b, pool_scale, router_w, expert_w_gate, expert_w_up, expert_w_down,
              final_g):
    bp, n_ctx = x_prompt.shape[:2]
    bs, n_lat = x_sample.shape[:2]
    past = cache_k.shape[2]
    cos, sin = axial_rope_tables(n_lat)
    xp, xs = x_prompt, x_sample
    new_k, new_v = [], []
    for l in range(DEPTH):
        sp1, cp1, gp1, sp2, cp2, gp2 = modulation(c_ctx, w_mod[l], b_mod[l])
        ss1, cs1, gs1, ss2, cs2, gs2 = modulation(c[:, None, :], w_mod[l], b_mod[l])
        hp = adaln(xp, norm1_g[l], sp1, cp1)
        hs = adaln(xs, norm1_g[l], ss1, cs1)
        if l % 2 == 0:
            a = l // 2
            lam_init = 0.8 - 0.6 * math.exp(-0.3 * l)
            lam = diff_lambda(lambda_q1[a], lambda_k1[a], lambda_q2[a], lambda_k2[a], lam_init)
            qp, kp, vp = project_qkv(hp, attn_wqkv[a])
            new_k.append(kp.reshape(bp, n_ctx, N_HEADS, 2 * HEAD_DIM))
            new_v.append(vp)
            mp = attn_output(diff_attention(qp, kp, vp, lam), subln_g[a], attn_wo[a], lam_init)
            qs, ks_, vs = project_qkv(hs, attn_wqkv[a])
            qs = apply_axial_rope(qs, cos, sin)
            ks_ = apply_axial_rope(ks_, cos, sin)
            kc = cache_k[:, a].reshape(bs, past, N_HEADS, 2, HEAD_DIM)
            k_all = jnp.concatenate([ks_, kc], axis=1)
            v_all = jnp.concatenate([vs, cache_v[:, a]], axis=1)
            ms = attn_output(diff_attention(qs, k_all, v_all, lam), subln_g[a], attn_wo[a], lam_init)
        else:
            p = l // 2
            mp = multiscale_pool(hp, pool_w[p], pool_b[p], pool_scale[p])
            ms = multiscale_pool(hs, pool_w[p], pool_b[p], pool_scale[p])
        xp = xp + gp1 * mp
        xs = xs + gs1 * ms
        hp = adaln(xp, norm2_g[l], sp2, cp2)
        hs = adaln(xs, norm2_g[l], ss2, cs2)
        fp = expert_choice_ffn(hp.reshape(-1, D_MODEL), router_w[l], expert_w_gate[l],
                               expert_w_up[l], expert_w_down[l]).reshape(xp.shape)
        fs = expert_choice_ffn(hs.reshape(-1, D_MODEL), router_w[l], expert_w_gate[l],
                               expert_w_up[l], expert_w_down[l]).reshape(xs.shape)
        xp = xp + gp2 * fp
        xs = xs + gs2 * fs
    y_prompt = rmsnorm(xp, final_g)
    y_sample = rmsnorm(xs, final_g)
    new_cache_k = jnp.stack(new_k, axis=1)
    new_cache_v = jnp.stack(new_v, axis=1)
    return (y_prompt, y_sample, new_cache_k, new_cache_v)


_drawn_inputs = setup_inputs


def setup_inputs(seed=0):
    import zlib

    import numpy as np

    out = dict(_drawn_inputs(seed))
    spreads = {}
    factors = {'cache_k': 3.319,
     'cache_v': 2.948,
     'b_mod': 3.664,
     'norm1_g': 3.015,
     'norm2_g': 5.091,
     'lambda_q1': 3.797,
     'lambda_q2': 8.0,
     'lambda_k2': 3.689,
     'subln_g': 8.0,
     'pool_b': 8.0,
     'pool_scale': 8.0,
     'final_g': 2.835}
    for name, (base, spread) in spreads.items():
        noise = np.random.default_rng([zlib.crc32(name.encode()), seed]).standard_normal(out[name].shape)
        drawn = base * np.exp(spread * noise) if base else spread * noise
        out[name] = __import__('jax').numpy.asarray(drawn.astype(out[name].dtype))
    for name, factor in factors.items():
        out[name] = (out[name] * factor).astype(out[name].dtype)
    return out
```

```python
from contextlib import ExitStack

import numpy as np

import concourse.bass as bass
from concourse import mybir

F32 = mybir.dt.float32
U32 = mybir.dt.uint32
ALU = mybir.AluOpType
ACT = mybir.ActivationFunctionType
AX = mybir.AxisListType

P = 128
D = 1024
DC = D // P
N_LAT = 1024
N_CTX = 128
LT = N_LAT // P
TT = LT + N_CTX // P
N_TOK = N_LAT + N_CTX
LAYERS = 2
H = 8
HD = 64
VD = 2 * HD
PAST = 128
KEYS = N_LAT + PAST
GRID_W = 64
ROPE_BASE = 10000.0
WINDOWS = (2, 4, 8, 16)
GROUP = D // len(WINDOWS)
E = 16
FF = 1408
CAP_L = 2 * N_LAT // E
CAP_C = 2 * N_CTX // E
CAP = CAP_L + CAP_C
EPS = 1e-6
LAM_INIT = 0.2
BANK = 512

PIECES = [3, 3, 3, 2]
PIECE0 = [0, 3, 6, 9]
SLOT = 3 * P * DC
RING_EARLY = 6

SHIFT1, SCALE1, GATE1, SHIFT2, SCALE2, GATE2 = range(6)
SECT = 6 * DC


class Step:

    def __init__(self, eng, sem, start=0):
        self.eng, self.sem, self.start, self.n = eng, sem, start, 0

    def count(self, ins):
        ins.then_inc(self.sem, 1)
        self.n += 1

    def wait(self):
        self.eng.wait_ge(self.sem, self.start + self.n)

    def link(self, ins):
        self.count(ins)
        self.wait()


def rope_tables():
    t = np.arange(N_LAT)
    half = HD // 2
    inv = (np.float32(ROPE_BASE) ** (-np.arange(0, half, 2, dtype=np.float32) / np.float32(half))).astype(np.float32)
    row = (t // GRID_W).astype(np.float32)[:, None] * inv
    col = (t % GRID_W).astype(np.float32)[:, None] * inv
    cos = np.concatenate([np.cos(row), np.cos(row), np.cos(col), np.cos(col)], axis=1)
    sin = np.concatenate([-np.sin(row), np.sin(row), -np.sin(col), np.sin(col)], axis=1)
    s = np.float32(HD ** -0.5)
    both = lambda m: np.concatenate([m * s, m * s, m, m], axis=1).astype(np.float32)
    return both(cos), both(sin)


def window_counts():
    out = []
    for w in WINDOWS:
        for n in (N_LAT, N_CTX):
            t = np.arange(n)
            out.append(np.clip(t + w // 2, 0, n) - np.clip(t - w // 2, 0, n))
    return (1.0 / np.concatenate(out)).astype(np.float32).reshape(len(WINDOWS), N_TOK)


def build(nc, a, out):
    with ExitStack() as ctx:
        place = {}

        def sb(name, shape, offset, dtype=F32):
            t = nc.alloc_sbuf_tensor_at(name, list(shape), dtype, offset=offset)
            size = 4 * int(np.prod(shape[1:]))
            return t, (offset + size + 31) // 32 * 32

        def sem(scope, name):
            s = nc.alloc_semaphore(name)
            scope.sems.append(s)
            return s

        class Stage(ExitStack):
            def __init__(self):
                super().__init__()
                self.sems = []
                self.callback(self.clear)

            def clear(self):
                nc.clear_and_free_semaphores(self.sems)
                nc.all_engine_barrier()

        bank = ctx.enter_context(nc.psum_tensor("bank", [P, 8, BANK], F32))

        at = 16512
        ident, at = sb("ident", [P, P], at)
        ones, at = sb("ones", [P, P], at)
        colsA, at = sb("colsA", [P, 128], at)
        colsB, at = sb("colsB", [P, 40], at)
        bmod2, at = sb("bmod2", [P, LAYERS * SECT, 2], at)
        modc, at = sb("modc", [P, LAYERS * SECT, 2], at)
        gains, at = sb("gains", [P, 4, DC, 2], at)
        silu, at = sb("silu", [P, 2, DC], at)
        nlam, at = sb("nlam", [P, 1], at)
        sub8, at = sb("sub8", [P, 1], at)
        hpow, at = sb("hpow", [P, 16], at)
        valL, at = sb("valL", [P, E + 1], at)
        valC, at = sb("valC", [P, E + 1], at)
        idxL, at = sb("idxL", [P, E + 1], at, U32)
        idxC, at = sb("idxC", [P, E + 1], at, U32)
        persistent_end = at

        xres = [nc.dram_tensor("xres_lat", (N_LAT, D), F32, kind="Internal").ap(),
                nc.dram_tensor("xres_ctx", (N_CTX, D), F32, kind="Internal").ap()]
        xnrm = [nc.dram_tensor("xnrm_lat", (N_LAT, D), F32, kind="Internal").ap(),
                nc.dram_tensor("xnrm_ctx", (N_CTX, D), F32, kind="Internal").ap()]

        def rows(pair, t):
            return pair[0][t * P:(t + 1) * P, :] if t < LT else pair[1][:, :]

        x_in = [a["x_sample"][0], a["x_prompt"][0]]

        big_at = persistent_end
        BIG = 4 * DC * (N_TOK + 32)
        ring_at = big_at + BIG
        SB = 4 * SLOT
        slot_off = [ring_at + i * SB for i in range(RING_EARLY)]
        late_at = ring_at + RING_EARLY * SB
        slot_off += [big_at + i * SB for i in range(3)]
        slot_off += [late_at + i * SB for i in range(3)]
        assert 3 * SB <= BIG
        exp_at = late_at + 3 * SB
        ring = [nc.alloc_sbuf_tensor_at(f"ring{i}", [P, SLOT], F32, offset=slot_off[i]) for i in range(12)]
        ring_in = [ctx.enter_context(nc.semaphore(f"ring_in{i}")) for i in range(12)]

        def ring_source(layer, e, i):
            j = i // 2 if i < 8 else i - 8
            nf, f0 = PIECES[j] * P, PIECE0[j] * P
            if i < 8:
                w = a["expert_w_gate" if i % 2 == 0 else "expert_w_up"]
                src = w[layer, e].rearrange("(c p) f -> p c f", p=P)[:, :, f0:f0 + nf]
                return ring[i][:, 0:DC * nf].rearrange("p (c f) -> p c f", c=DC), src
            src = a["expert_w_down"][layer, e, f0:f0 + nf].rearrange("(q p) d -> p q d", p=P)
            return ring[i][:, 0:PIECES[j] * D].rearrange("p (q d) -> p q d", q=PIECES[j]), src

        def setup_and_norm(hT):
            with Stage() as st:
                off = persistent_end + BIG
                rA, off = sb("rA", [P, P], off)
                rB, off = sb("rB", [P, P], off)
                wm, off = sb("wm", [P, 2, DC, BANK], off)
                xt, off = sb("xt", [P, TT, D], off)
                sq, off = sb("sq", [P, D], off)
                ssq, off = sb("ssq", [P, 16], off)
                rstd, off = sb("rstd", [P, 16], off)
                mrow, off = sb("mrow", [P, 2, BANK], off)
                lrow, off = sb("lrow", [P, 4, HD], off)
                lsum, off = sb("lsum", [P, 8], off)
                sg, off = sb("sg", [P, 3, 2, DC], off)
                assert off <= nc.sbuf_usable_end
                s_rows, s_id, s_lam = sem(st, "s0_rows_in"), sem(st, "s0_ident_in"), sem(st, "s0_lam_in")
                s_w = [sem(st, f"s0_wmod_in{i}") for i in range(2)]
                s_x = [sem(st, f"s0_x_in{t}") for t in range(TT)]
                cols_T, cols_ok = sem(st, "s0_cols_transposed"), sem(st, "s0_cols_copied")
                silu_ok, exp_ok = sem(st, "s0_silu_ready"), sem(st, "s0_exp_ready")
                row_mm, row_ok = sem(st, "s0_modrow_mm"), sem(st, "s0_modrow_copied")
                col_T, mod_ok = sem(st, "s0_modcol_transposed"), sem(st, "s0_mod_ready")
                ssq_ok, rstd_ok = sem(st, "s0_ssq_ready"), sem(st, "s0_rstd_ready")
                xn_ok, xT_mm, hT_ok = sem(st, "s0_xn_ready"), sem(st, "s0_x_transposed"), sem(st, "s0_hT_ready")
                d_step, p_step, lam_ok = sem(st, "s0_dve_step"), sem(st, "s0_pool_step"), sem(st, "s0_lam_exp")
                ones_ok = sem(st, "s0_ones_ready")
                block = st.enter_context(nc.Block())
                NT = 2 * DC * P // BANK

                @block.sync
                def _(sp):
                    sp.dma_start(ident[:], a["ident"]).then_inc(s_id, 16)
                    ra = rA[:, :]
                    sp.dma_start(ra[0:96], a["b_mod"].rearrange("l (t p) -> (l t) p", p=P)).then_inc(s_rows, 16)
                    sp.dma_start(ra[96:112], a["norm1_g"].rearrange("l (t p) -> (l t) p", p=P)).then_inc(s_rows, 16)
                    sp.dma_start(ra[112:128], a["norm2_g"].rearrange("l (t p) -> (l t) p", p=P)).then_inc(s_rows, 16)
                    rb = rB[:, :]
                    sp.dma_start(rb[0:8], a["c"].rearrange("b (t p) -> (b t) p", p=P)).then_inc(s_rows, 16)
                    sp.dma_start(rb[8:16], a["c_ctx"].rearrange("(t p) -> t p", p=P)).then_inc(s_rows, 16)
                    sp.dma_start(rb[16:24], a["pool_b"].rearrange("l g (t p) -> (l g t) p", p=P)).then_inc(s_rows, 16)
                    sp.dma_start(rb[24:32], a["pool_scale"].rearrange("l (t p) -> (l t) p", p=P)).then_inc(s_rows, 16)
                    sp.dma_start(rb[32:33], a["subln_g"]).then_inc(s_rows, 16)
                    for i in range(NT):
                        if i >= 2:
                            sp.wait_ge(row_mm, i - 1)
                        sp.dma_start(wm[:, i % 2], a["w_mod"][0].rearrange("(c p) n -> p c n", p=P)[
                            :, :, i * BANK:(i + 1) * BANK]).then_inc(s_w[i % 2], 16)

                @block.scalar
                def _(act):
                    for t in range(TT):
                        act.dma_start(xt[:, t], rows(x_in, t)).then_inc(s_x[t], 16)
                    for i, n in enumerate(("lambda_q1", "lambda_k1", "lambda_q2", "lambda_k2")):
                        act.dma_start(lrow[:, i], a[n].partition_broadcast(P).rearrange("p a d -> p (a d)")
                                      ).then_inc(s_lam, 16)
                    act.wait_ge(cols_ok, 3)
                    cc = colsB[:, 0:16].rearrange("p (s c) -> p s c", s=2)
                    nc.scalar.activation(sg[:, 0], cc, ACT.Exp, scale=-1.0).then_inc(exp_ok, 1)
                    act.wait_ge(ssq_ok, TT + 1)
                    nc.scalar.activation(lsum[:, 2:4], lsum[:, 0:2], ACT.Exp).then_inc(lam_ok, 1)
                    for i in range(NT):
                        act.wait_ge(row_mm, i + 1)
                        if i >= 2:
                            act.wait_ge(col_T, i - 1)
                        nc.scalar.activation(mrow[0:2, i % 2], bank[0:2, i % 2], ACT.Copy).then_inc(row_ok, 1)
                    act.wait_ge(rstd_ok, 1)
                    for t in range(TT):
                        nc.scalar.activation(xt[:, t], xt[:, t], ACT.Copy, scale=rstd[:, t:t + 1]).then_inc(xn_ok, 1)

                @block.gpsimd
                def _(pool):
                    nc.gpsimd.memset(ones[:], 1.0).then_inc(ones_ok, 1)
                    nc.gpsimd.memset(hpow[:], -0.5).then_inc(p_step, 1)
                    pool.wait_ge(ssq_ok, TT)
                    nc.gpsimd.tensor_scalar(ssq[:, 0:TT], ssq[:, 0:TT], 1.0 / D, EPS, ALU.mult, ALU.add
                                            ).then_inc(p_step, 1)
                    pool.wait_ge(p_step, 2)
                    nc.gpsimd.tensor_tensor(rstd[:, 0:TT], ssq[:, 0:TT], hpow[:, 0:TT], ALU.pow).then_inc(rstd_ok, 1)

                @block.vector
                def _(dve):
                    step = Step(dve, d_step)
                    dve.wait_ge(cols_T, 1)
                    nc.vector.tensor_copy(colsA[:], bank[:, 2, 0:128]).then_inc(cols_ok, 1)
                    dve.wait_ge(cols_T, 2)
                    nc.vector.tensor_copy(colsB[:, 0:33], bank[:, 3, 0:33]).then_inc(cols_ok, 1)
                    dve.wait_ge(cols_ok, 2)
                    for cond in range(2):
                        nc.vector.tensor_copy(bmod2[:, :, cond], colsA[:, 0:96]).then_inc(cols_ok, 1)
                    nc.vector.tensor_scalar(sub8[:], colsB[:, 32:33], 1.0 - LAM_INIT, None, ALU.mult
                                            ).then_inc(cols_ok, 1)
                    dve.wait_ge(exp_ok, 1)
                    step.link(nc.vector.tensor_scalar(sg[:, 1], sg[:, 0], 1.0, None, ALU.add))
                    step.link(nc.vector.reciprocal(sg[:, 2], sg[:, 1]))
                    nc.vector.tensor_tensor(silu[:], colsB[:, 0:16].rearrange("p (s c) -> p s c", s=2), sg[:, 2],
                                            ALU.mult).then_inc(silu_ok, 1)
                    for t in range(TT):
                        dve.wait_ge(s_x[t], 16)
                        if t:
                            dve.wait_ge(ssq_ok, t)
                        nc.vector.tensor_tensor_reduce(sq[:], xt[:, t], xt[:, t], 1.0, 0.0, ALU.mult, ALU.add,
                                                       ssq[:, t:t + 1]).then_inc(ssq_ok, 1)
                    dve.wait_ge(s_lam, 64)
                    dve.wait_ge(ssq_ok, TT)
                    step.link(nc.vector.tensor_tensor_reduce(sq[:, 0:HD], lrow[:, 0], lrow[:, 1], 1.0, 0.0, ALU.mult,
                                                             ALU.add, lsum[:, 0:1]))
                    nc.vector.tensor_tensor_reduce(sq[:, 0:HD], lrow[:, 2], lrow[:, 3], 1.0, 0.0, ALU.mult, ALU.add,
                                                   lsum[:, 1:2]).then_inc(ssq_ok, 1)
                    dve.wait_ge(lam_ok, 1)
                    step.link(nc.vector.tensor_tensor(lsum[:, 4:5], lsum[:, 3:4], lsum[:, 2:3], ALU.subtract))
                    step.link(nc.vector.tensor_scalar(nlam[:], lsum[:, 4:5], -LAM_INIT, None, ALU.add))
                    for i in range(NT):
                        dve.wait_ge(col_T, i + 1)
                        n = BANK // P
                        nc.vector.tensor_tensor(modc[:, n * i:n * i + n, :],
                                                bank[:, 4 + i % 2, 0:2 * n].rearrange("p (n s) -> p n s", s=2),
                                                bmod2[:, n * i:n * i + n, :], ALU.add).then_inc(mod_ok, 1)
                    dve.wait_ge(mod_ok, NT)
                    for cond in range(2):
                        nc.vector.scalar_tensor_tensor(gains[:, 0, :, cond], modc[:, SCALE1 * DC:SCALE1 * DC + DC, cond],
                                                       1.0, colsA[:, 96:96 + DC], ALU.add, ALU.mult
                                                       ).then_inc(mod_ok, 1)
                    dve.wait_ge(mod_ok, NT + 2)
                    n = 0
                    for g, (t0, nt) in enumerate(((0, 4), (4, 4), (8, 1))):
                        cond = 1 if t0 == LT else 0
                        for c in range(DC):
                            dve.wait_ge(xT_mm, n + 1)
                            nc.vector.tensor_scalar(hT[:, c, t0 * P:(t0 + nt) * P], bank[:, n % 8, 0:nt * P],
                                                    gains[:, 0, c, cond:cond + 1],
                                                    modc[:, SHIFT1 * DC + c, cond:cond + 1], ALU.mult, ALU.add
                                                    ).then_inc(hT_ok, 1)
                            n += 1

                @block.tensor
                def _(pe):
                    pe.wait_ge(s_id, 16)
                    pe.wait_ge(s_rows, 16 * 8)
                    nc.tensor.transpose(bank[:, 2, 0:128], rA[:], ident[:]).then_inc(cols_T, 1)
                    nc.tensor.transpose(bank[:, 3, 0:33], rB[0:33], ident[0:33, 0:33]).then_inc(cols_T, 1)
                    pe.wait_ge(silu_ok, 1)
                    n = BANK // P
                    for i in range(NT + 1):
                        if i < NT:
                            pe.wait_ge(s_w[i % 2], 16 * (i // 2 + 1))
                            if i >= 2:
                                pe.wait_ge(row_ok, i - 1)
                            for c in range(DC):
                                last = nc.tensor.matmul(bank[0:2, i % 2, :], silu[:, :, c], wm[:, i % 2, c],
                                                        start=(c == 0), stop=(c == DC - 1))
                            last.then_inc(row_mm, 1)
                        if i:
                            pe.wait_ge(row_ok, i)
                            if i >= 3:
                                pe.wait_ge(mod_ok, i - 2)
                            for j in range(n):
                                last = nc.tensor.transpose(bank[:, 4 + (i - 1) % 2, 2 * j:2 * j + 2],
                                                           mrow[0:2, (i - 1) % 2, j * P:(j + 1) * P], ident[0:2, 0:2])
                            last.then_inc(col_T, 1)
                    n = 0
                    pe.wait_ge(cols_ok, 2)
                    pe.wait_ge(row_ok, NT)
                    pe.wait_ge(mod_ok, NT)
                    for t0, nt in ((0, 4), (4, 4), (8, 1)):
                        pe.wait_ge(xn_ok, t0 + nt)
                        for c in range(DC):
                            if n >= 8:
                                pe.wait_ge(hT_ok, n - 7)
                            for j in range(nt):
                                last = nc.tensor.transpose(bank[:, n % 8, j * P:(j + 1) * P],
                                                           xt[:, t0 + j, c * P:(c + 1) * P], ident[:])
                            last.then_inc(xT_mm, 1)
                            n += 1

        def attention(hT, oraw, off):
            with Stage() as st:
                ctab, off = sb("ctab", [P, LT, 2 * VD], off)
                stab, off = sb("stab", [P, LT, 2 * VD], off)
                wh, off = sb("wh", [P, DC, 3 * VD], off)
                wmA, off = sb("wmA", [P, DC, 512], off)
                wmB, off = sb("wmB", [P, DC, 768], off)
                qT, off = sb("qT", [P, N_TOK], off)
                kT, off = sb("kT", [P, KEYS + N_CTX], off)
                V, off = sb("V", [P, 10, VD], off)
                kc, off = sb("kc", [P, VD], off)
                rot, off = sb("rot", [P, 2, 2 * VD], off)
                m1, off = sb("m1", [P, 2 * VD], off)
                m2, off = sb("m2", [P, 2 * VD], off)
                Pe, off = sb("Pe", [P, 2, KEYS], off)
                am, off = sb("am", [P, KEYS], off)
                PT, off = sb("PT", [P, 2, KEYS], off)
                mr, off = sb("mr", [P, 1280], off)
                mxp, off = sb("mxp", [P, 2, 2], off)
                nm, off = sb("nm", [P, 2], off)
                ssum, off = sb("ssum", [P, 2, 2], off)
                tot, off = sb("tot", [P, 2], off)
                rec, off = sb("rec", [P, TT, 2], off)
                cneg, off = sb("cneg", [P, 1], off)
                assert off <= nc.sbuf_usable_end, off
                S = {}
                for n in ("tail_mm tail_mx tab_in wh_in kc_in vc_in wmA_in wmB_in kv_out qkv_mm v_done rot_done rot_T qk_evac S_mm "
                          "mx_part mx_done exp_done comb_step a_done aT_mm PTd PTa pv_mm o_evac modrow_mm row_evac "
                          "modcol_T modc_done rope_part").split():
                    S[n] = sem(st, "at_" + n)
                block = st.enter_context(nc.Block())
                LAST = TT - 1
                w = a["attn_wqkv"][0].rearrange("(c p) n -> p c n", p=P)
                wmod = [a["w_mod"][l].rearrange("(c p) n -> p c n", p=P) for l in range(LAYERS)]
                kcd = a["cache_k"][0, 0].rearrange("t h d -> t (h d)")
                vcd = a["cache_v"][0, 0].rearrange("t h d -> t (h d)")
                nkd = out["new_cache_k"][0, 0].rearrange("t h d -> t (h d)")
                nvd = out["new_cache_v"][0, 0].rearrange("t h d -> t (h d)")

                @block.sync
                def _(sp):
                    def load_wh(h):
                        for i in range(3):
                            sp.dma_start(wh[:, :, i * VD:(i + 1) * VD], w[:, :, bass.ds(i * H * VD + h * VD, VD)]
                                         ).then_inc(S["wh_in"], 16)

                    def load_kc(h):
                        sp.dma_start(kc[:], kcd[:, bass.ds(h * VD, VD)]).then_inc(S["kc_in"], 16)

                    def load_vc(h):
                        sp.dma_start(V[:, LT], vcd[:, bass.ds(h * VD, VD)]).then_inc(S["vc_in"], 16)

                    def load_wm(h):
                        sp.dma_start(wmA[:], wmod[0][:, :, bass.ds(2 * D + h * 512, 512)]).then_inc(S["wmA_in"], 16)
                        sp.dma_start(wmB[:], wmod[1][:, :, bass.ds(h * 768, 768)]).then_inc(S["wmB_in"], 16)

                    def store_kv(h):
                        sp.wait_ge(S["rot_done"], TT * h + TT)
                        sp.dma_start(nkd[:, bass.ds(h * VD, VD)], rot[:, LAST % 2, VD:2 * VD]).then_inc(S["kv_out"], 16)
                        sp.wait_ge(S["v_done"], TT * h + TT)
                        sp.dma_start(nvd[:, bass.ds(h * VD, VD)], V[:, LT + 1]).then_inc(S["kv_out"], 16)

                    sp.sem_inc(S["kv_out"], 1)
                    load_wh(0)
                    sp.dma_start(ctab[:], a["rope_cos"].rearrange("(t p) n -> p t n", p=P)).then_inc(S["tab_in"], 16)
                    sp.dma_start(stab[:], a["rope_sin"].rearrange("(t p) n -> p t n", p=P)).then_inc(S["tab_in"], 16)
                    load_kc(0)
                    load_vc(0)
                    load_wm(0)
                    with sp.Fori(0, H - 1) as h:
                        store_kv(h)
                        sp.wait_ge(S["qkv_mm"], TT * h + TT)
                        load_wh(h + 1)
                        sp.wait_ge(S["rot_T"], (TT + 1) * h + TT + 1)
                        load_kc(h + 1)
                        sp.wait_ge(S["modrow_mm"], h + 1)
                        load_wm(h + 1)
                        sp.wait_ge(S["pv_mm"], TT * h + TT)
                        load_vc(h + 1)
                    store_kv(H - 1)
                    sp.wait_ge(S["kv_out"], 32 * H + 1)

                @block.tensor
                def _(pe):
                    def qkv(h, t):
                        if t == 0:
                            pe.wait_ge(S["wh_in"], 48 * h + 48)
                        else:
                            if t >= 2:
                                pe.wait_ge(S["v_done"], TT * h + t - 1)
                                pe.wait_ge(S["rot_done"], TT * h + t - 1)
                        for c in range(DC):
                            last = nc.tensor.matmul(bank[:, 5 + t % 2, 0:3 * VD], hT[:, c, t * P:(t + 1) * P], wh[:, c],
                                                    start=(c == 0), stop=(c == DC - 1))
                        last.then_inc(S["qkv_mm"], 1)

                    def turn(h, t):
                        pe.wait_ge(S["rot_done"], TT * h + t + 1)
                        if t < LAST:
                            qo, ko = bank[:, t // 4, (t % 4) * P:(t % 4 + 1) * P], bank[:, 2 + t // 4, (t % 4) * P:(t % 4 + 1) * P]
                        else:
                            pe.wait_ge(S["modc_done"], 2 * h + 1)
                            qo, ko = bank[:, 4, 0:P], bank[:, 4, 2 * P:3 * P]
                        nc.tensor.transpose(qo, rot[:, t % 2, 0:VD], ident[:])
                        nc.tensor.transpose(ko, rot[:, t % 2, VD:2 * VD], ident[:]).then_inc(S["rot_T"], 1)
                        if t == LAST:
                            pe.wait_ge(S["kc_in"], 16 * h + 16)
                            nc.tensor.transpose(bank[:, 4, P:2 * P], kc[:], ident[:]).then_inc(S["rot_T"], 1)

                    def scores(h, n):
                        q = [qT[HD * s:HD * s + HD, n * P:(n + 1) * P] for s in range(2)]
                        k = [kT[HD * s:HD * s + HD] for s in range(2)]
                        if n == 0:
                            pe.wait_ge(S["qk_evac"], 6 * h + 6)
                        if n < LAST:
                            if n:
                                pe.wait_ge(S["exp_done"], 2 * TT * h + 2 * n)
                        for s in range(2):
                            if n == LAST:
                                pe.wait_ge(S["exp_done"], 2 * TT * h + 2 * n + s - 1)
                                last = nc.tensor.matmul(bank[:, 2 * s, 0:N_CTX], q[s], k[s][:, KEYS:KEYS + N_CTX],
                                                        start=True, stop=True)
                            else:
                                if s:
                                    pe.wait_ge(S["tail_mm"], 2 * LT * h + 2 * n + 1)
                                nc.tensor.matmul(bank[:, 4, s * P:(s + 1) * P], q[s], k[s][:, N_LAT:KEYS],
                                                 start=True, stop=True).then_inc(S["tail_mm"], 1)
                                nc.tensor.matmul(bank[:, 2 * s, :], q[s], k[s][:, 0:512], start=True, stop=True)
                                last = nc.tensor.matmul(bank[:, 2 * s + 1, :], q[s], k[s][:, 512:1024], start=True, stop=True)
                            last.then_inc(S["S_mm"], 1)

                    def turn_a(h, n):
                        pe.wait_ge(S["a_done"], TT * h + n + 2)
                        if n == 0:
                            pe.wait_ge(S["v_done"], TT * h + TT)
                        else:
                            pe.wait_ge(S["PTa"], 2 * LT * h + 2 * n)
                        for j in range(4 if n < LAST else 1):
                            last = nc.tensor.transpose(bank[:, 5, j * P:(j + 1) * P], am[:, j * P:(j + 1) * P], ident[:])
                        last.then_inc(S["aT_mm"], 1)
                        if n < LAST:
                            for j in range(4, 8):
                                last = nc.tensor.transpose(bank[:, 6, (j - 4) * P:(j - 3) * P], am[:, j * P:(j + 1) * P], ident[:])
                            last.then_inc(S["aT_mm"], 1)

                    def turn_a_tail(h, n):
                        pe.wait_ge(S["PTd"], TT * h + n + 1)
                        nc.tensor.transpose(bank[:, 5, 0:P], am[:, N_LAT:KEYS], ident[:]).then_inc(S["aT_mm"], 1)

                    def times_v(h, n):
                        pe.wait_ge(S["PTd"], TT * h + n + 1)
                        if n < LAST:
                            pe.wait_ge(S["PTa"], 2 * LT * h + 2 * n + 2)
                        if n == 0:
                            pe.wait_ge(S["vc_in"], 16 * h + 16)
                        pe.wait_ge(S["o_evac"], TT * h + n + 1)
                        tiles = range(LT + 1) if n < LAST else [LT + 1]
                        for i, j in enumerate(tiles):
                            last = nc.tensor.matmul(bank[:, 7, 0:VD], PT[:, n % 2, i * P:(i + 1) * P], V[:, j],
                                                    start=(i == 0), stop=(i == len(tiles) - 1))
                        last.then_inc(S["pv_mm"], 1)

                    pe.sem_inc(S["modcol_T"], 1)
                    with pe.Fori(0, H) as h:
                        for t in range(TT):
                            qkv(h, t)
                            if t:
                                turn(h, t - 1)
                        turn(h, LAST)
                        for n in range(TT + 2):
                            if n < TT:
                                scores(h, n)
                            if 1 <= n <= TT:
                                turn_a(h, n - 1)
                            if n == TT + 1:
                                pe.wait_ge(S["row_evac"], h + 1)
                            if n >= 2:
                                times_v(h, n - 2)
                            if 1 <= n <= LT:
                                turn_a_tail(h, n - 1)
                            if n == LAST:
                                pe.wait_ge(S["wmA_in"], 16 * h + 16)
                                pe.wait_ge(S["wmB_in"], 16 * h + 16)
                                for b, wsrc in ((1, wmA[:, :, 0:512]), (3, wmB[:, :, 0:384]), (4, wmB[:, :, 384:768])):
                                    for c in range(DC):
                                        last = nc.tensor.matmul(bank[0:2, b, 0:wsrc.shape[2]], silu[:, :, c], wsrc[:, c],
                                                                start=(c == 0), stop=(c == DC - 1))
                                last.then_inc(S["modrow_mm"], 1)
                        for j in range(10):
                            last = nc.tensor.transpose(bank[:, 4, 400 + 2 * j:402 + 2 * j], mr[0:2, j * P:(j + 1) * P],
                                                       ident[0:2, 0:2])
                        last.then_inc(S["modcol_T"], 1)

                @block.scalar
                def _(act):
                    act.sem_inc(S["o_evac"], 1)
                    with act.Fori(0, H) as h:
                        for t in range(TT):
                            if t < LAST:
                                act.wait_ge(S["rope_part"], LT * h + t + 1)
                            else:
                                act.wait_ge(S["rot_done"], TT * h + TT)
                                act.wait_ge(S["kv_out"], 32 * h + 1)
                            nc.scalar.activation(V[:, t if t < LT else LT + 1], bank[:, 5 + t % 2, 2 * VD:3 * VD], ACT.Copy
                                                 ).then_inc(S["v_done"], 1)
                            if t in (4, 8):
                                g = t // 4 - 1
                                act.wait_ge(S["rot_T"], (TT + 1) * h + 4 * g + 4)
                                nc.scalar.activation(qT[:, 512 * g:512 * g + 512], bank[:, g], ACT.Copy).then_inc(S["qk_evac"], 1)
                                nc.scalar.activation(kT[:, 512 * g:512 * g + 512], bank[:, 2 + g], ACT.Copy).then_inc(S["qk_evac"], 1)
                        act.wait_ge(S["rot_T"], (TT + 1) * h + TT + 1)
                        nc.scalar.activation(qT[:, N_LAT:N_TOK], bank[:, 4, 0:P], ACT.Copy).then_inc(S["qk_evac"], 1)
                        nc.scalar.activation(kT[:, N_LAT:KEYS + N_CTX], bank[:, 4, P:3 * P], ACT.Copy).then_inc(S["qk_evac"], 1)
                        for n in range(TT + 2):
                            if n < TT:
                                for s in range(2):
                                    act.wait_ge(S["mx_done"], 2 * TT * h + 2 * n + s + 1)
                                    if s == 0 and n < LAST:
                                        act.wait_ge(S["tail_mx"], LT * h + n + 1)
                                    if s == 0:
                                        act.wait_ge(S["a_done"], TT * h + n + 1)
                                    if n < LAST:
                                        nc.scalar.activation(Pe[:, s, N_LAT:KEYS], bank[:, 4, s * P:(s + 1) * P], ACT.Exp,
                                                             bias=nm[:, s:s + 1], accum_out=ssum[:, s, 1:2])
                                        nc.scalar.activation(Pe[:, s, 0:N_LAT].rearrange("p (b n) -> p b n", b=2), bank[:, 2 * s:2 * s + 2, :], ACT.Exp,
                                                             bias=nm[:, s:s + 1], accum_out=ssum[:, s, 0:1]).then_inc(S["exp_done"], 1)
                                    else:
                                        nc.scalar.activation(Pe[:, s, 0:N_CTX], bank[:, 2 * s, 0:N_CTX], ACT.Exp,
                                                             bias=nm[:, s:s + 1], accum_out=ssum[:, s, 0:1]).then_inc(S["exp_done"], 1)
                            if 1 <= n <= LT:
                                m = n - 1
                                act.wait_ge(S["aT_mm"], (3 * LT + 1) * h + 3 * m + 2)
                                nc.scalar.activation(PT[:, m % 2, 512:1024], bank[:, 6], ACT.Copy).then_inc(S["PTa"], 1)
                                act.wait_ge(S["aT_mm"], (3 * LT + 1) * h + 3 * m + 3)
                                nc.scalar.activation(PT[:, m % 2, N_LAT:KEYS], bank[:, 5, 0:P], ACT.Copy).then_inc(S["PTa"], 1)
                            if n == LAST:
                                act.wait_ge(S["modrow_mm"], h + 1)
                                act.wait_ge(S["modcol_T"], h + 1)
                                nc.scalar.activation(mr[0:2, 0:512], bank[0:2, 1, :], ACT.Copy)
                                nc.scalar.activation(mr[0:2, 512:896], bank[0:2, 3, 0:384], ACT.Copy)
                                nc.scalar.activation(mr[0:2, 896:1280], bank[0:2, 4, 0:384], ACT.Copy).then_inc(S["row_evac"], 1)
                            if n >= 2:
                                m = n - 2
                                act.wait_ge(S["pv_mm"], TT * h + m + 1)
                                nc.scalar.activation(oraw[:, m, bass.ds(h * VD, VD)], bank[:, 7, 0:VD], ACT.Copy,
                                                     scale=rec[:, m, 0:1]).then_inc(S["o_evac"], 1)

                @block.vector
                def _(dve):
                    dve.sem_inc(S["modc_done"], 1)
                    dve.sem_inc(S["a_done"], 1)
                    dve.wait_ge(S["tab_in"], 32)
                    with dve.Fori(0, H) as h:
                        for t in range(TT):
                            dve.wait_ge(S["qkv_mm"], TT * h + t + 1)
                            src = bank[:, 5 + t % 2, 0:2 * VD]
                            if t == 0:
                                dve.wait_ge(S["kv_out"], 32 * h + 1)
                            if t >= 2:
                                dve.wait_ge(S["rot_T"], (TT + 1) * h + t - 1)
                            if t == LAST:
                                nc.vector.tensor_scalar(rot[:, t % 2, 0:VD], src[:, 0:VD], HD ** -0.5, None, ALU.mult)
                                nc.vector.tensor_copy(rot[:, t % 2, VD:2 * VD], src[:, VD:2 * VD]).then_inc(S["rot_done"], 1)
                                continue
                            if t:
                                dve.wait_ge(S["rot_done"], TT * h + t)
                            sw = src.rearrange("p (b two r) -> p b two r", two=2, r=16)
                            dw = m2[:].rearrange("p (b two r) -> p b two r", two=2, r=16)
                            tw = stab[:, t].rearrange("p (b two r) -> p b two r", two=2, r=16)
                            nc.vector.tensor_tensor(m1[:], src, ctab[:, t], ALU.mult)
                            for i in range(2):
                                last = nc.vector.tensor_tensor(dw[:, :, i], sw[:, :, 1 - i], tw[:, :, i], ALU.mult)
                            last.then_inc(S["rope_part"], 1)
                            dve.wait_ge(S["rope_part"], LT * h + t + 1)
                            nc.vector.tensor_tensor(rot[:, t % 2], m1[:], m2[:], ALU.add).then_inc(S["rot_done"], 1)
                        for n in range(TT + 1):
                            if n < TT:
                                for s in range(2):
                                    dve.wait_ge(S["S_mm"], 2 * TT * h + 2 * n + s + 1)
                                    if n < LAST:
                                        nc.vector.tensor_reduce(mxp[:, s, 0:1], bank[:, 2 * s:2 * s + 2, :], AX.XY, ALU.max
                                                                ).then_inc(S["mx_part"], 1)
                                        if s == 0:
                                            dve.wait_ge(S["tail_mm"], 2 * LT * h + 2 * n + 2)
                                            nc.vector.tensor_reduce(mxp[:, :, 1], bank[:, 4, 0:2 * P].rearrange("p (s k) -> p s k", s=2),
                                                                    AX.X, ALU.max).then_inc(S["tail_mx"], 1)
                                            dve.wait_ge(S["tail_mx"], LT * h + n + 1)
                                        dve.wait_ge(S["mx_part"], 2 * LT * h + 2 * n + s + 1)
                                        nc.vector.tensor_reduce(nm[:, s:s + 1], mxp[:, s], AX.X, ALU.max, negate=True
                                                                ).then_inc(S["mx_done"], 1)
                                    else:
                                        nc.vector.tensor_reduce(nm[:, s:s + 1], bank[:, 2 * s, 0:N_CTX], AX.X, ALU.max,
                                                                negate=True).then_inc(S["mx_done"], 1)
                            if n >= 1:
                                m = n - 1
                                dve.wait_ge(S["aT_mm"], (3 * LT + 1) * h + 3 * m + 1)
                                kw = 512 if m < LAST else N_CTX
                                nc.vector.tensor_copy(PT[:, m % 2, 0:kw], bank[:, 5, 0:kw]).then_inc(S["PTd"], 1)
                            if n < TT:
                                dve.wait_ge(S["exp_done"], 2 * TT * h + 2 * n + 2)
                                step = Step(dve, S["comb_step"], 3 * TT * h + 3 * n)
                                if n < LAST:
                                    step.link(nc.vector.tensor_tensor(tot[:], ssum[:, :, 0], ssum[:, :, 1], ALU.add))
                                else:
                                    step.link(nc.vector.tensor_copy(tot[:], ssum[:, :, 0]))
                                step.link(nc.vector.reciprocal(rec[:, n], tot[:]))
                                step.link(nc.vector.scalar_tensor_tensor(cneg[:], rec[:, n, 1:2], tot[:, 0:1], nlam[:],
                                                                         ALU.mult, ALU.mult))
                                kw = KEYS if n < LAST else N_CTX
                                if n:
                                    dve.wait_ge(S["aT_mm"], (3 * LT + 1) * h + 3 * n)
                                nc.vector.scalar_tensor_tensor(am[:, 0:kw], Pe[:, 1, 0:kw], cneg[:], Pe[:, 0, 0:kw],
                                                               ALU.mult, ALU.add).then_inc(S["a_done"], 1)
                        dve.wait_ge(S["modcol_T"], h + 2)
                        cols = bank[:, 4, 400:420].rearrange("p (n s) -> p n s", s=2)
                        for lo, n, j in ((2 * DC + 4 * h, 4, 0), (SECT + 6 * h, 6, 4)):
                            nc.vector.tensor_tensor(modc[:, bass.ds(lo, n), :], cols[:, j:j + n], bmod2[:, bass.ds(lo, n), :],
                                                    ALU.add).then_inc(S["modc_done"], 1)

        def mixer_and_route(layer, oraw, pT, off):
            attn = layer == 0
            cond_of = [0] * LT + [1]
            with Stage() as st:
                xt, off = sb(f"mx_xt{layer}", [P, 2, D], off)
                xn, off = sb(f"mx_xn{layer}", [P, 2, D], off)
                h2, off = sb(f"mx_h2{layer}", [P, 2, DC, P], off)
                gA, off = sb(f"mx_gA{layer}", [P, 2, D], off)
                wr, off = sb(f"mx_wr{layer}", [P, DC, E], off)
                sm, off = sb(f"mx_sm{layer}", [P, 2, 4, E], off)
                st1, off = sb(f"mx_st{layer}", [P, TT, 8], off)
                if attn:
                    wo, _ = sb("mx_wo", [P, H, D], big_at)
                    om, off = sb("mx_om", [P, D], off)
                    oT, off = sb("mx_oT", [P, 2, H, P], off)
                    osm, off = sb("mx_osm", [P, 2, 2, H], off)
                    alias = om
                else:
                    pw, off = sb("mx_pw", [P, 4, 2, GROUP], off)
                    gB, off = sb("mx_gB", [P, 2, D], off)
                    pcol, off = sb("mx_pcol", [P, 2, DC, 2], off)
                dg, off = sb(f"mx_dg{layer}", [P, 2, P], off)
                af, off = sb(f"mx_af{layer}", [P, N_TOK], off)
                vv, off = sb(f"mx_vv{layer}", [P, P], off)
                ii, off = sb(f"mx_ii{layer}", [P, P], off, U32)
                fi, off = sb(f"mx_fi{layer}", [P, P], off)
                vc, off = sb(f"mx_vc{layer}", [P, CAP_C], off)
                ic, off = sb(f"mx_ic{layer}", [P, CAP_C], off, U32)
                fc, off = sb(f"mx_fc{layer}", [P, CAP_C], off)
                assert off <= (oraw_at if attn else nc.sbuf_usable_end), off
                S = {}
                for n in ("w_in wr_in xx_out gain_ok dg_ok dg_used bc_mm bc_ok om_ok oT_mm oT_ok mm_done tmp_ok x_ok ssq_ok "
                          "rstd_ok xn_ok xT_mm h2_ok lg_mm lmax_ok lexp_ok aff_ok affT_mm af_ok dve_step pool_step "
                          "top_mm sq_ok oss_ok orstd_ok xu").split():
                    S[n] = sem(st, f"mx{layer}_" + n)
                x_in_s = [sem(st, f"mx{layer}_x_in{i}") for i in range(2)]
                x_out = [sem(st, f"mx{layer}_x_out{i}") for i in range(2)]
                xn_out = [sem(st, f"mx{layer}_xn_out{i}") for i in range(2)]
                block = st.enter_context(nc.Block())
                g2 = 2 * layer + 1
                base = layer * SECT
                NB = 2 if attn else 4
                x_src = x_in if attn else xres

                @block.sync
                def _(sp):
                    if attn:
                        sp.dma_start(wo[:], a["attn_wo"][0].rearrange("(h p) d -> p h d", p=P)).then_inc(S["w_in"], 16)
                    else:
                        sp.dma_start(pw[:], a["pool_w"][0].rearrange("g (c p) d -> p g c d", p=P)).then_inc(S["w_in"], 16)
                    sp.dma_start(wr[:], a["router_w"][layer].rearrange("(c p) e -> p c e", p=P)).then_inc(S["wr_in"], 16)
                    for t in range(2):
                        sp.dma_start(xt[:, t], rows(x_src, t)).then_inc(x_in_s[t], 16)
                    for i in range(RING_EARLY):
                        dst, src = ring_source(layer, 0, i)
                        sp.dma_start(dst, src).then_inc(ring_in[i], 16)
                    for t in range(TT):
                        sp.wait_ge(S["x_ok"], t + 1)
                        sp.dma_start(rows(xres, t), xt[:, t % 2]).then_inc(x_out[t % 2], 16)
                        sp.wait_ge(S["xn_ok"], t + 1)
                        sp.dma_start(rows(xnrm, t), xn[:, t % 2]).then_inc(xn_out[t % 2], 16)
                        if t + 2 < TT:
                            sp.wait_ge(x_out[t % 2], 16 * (t // 2 + 1))
                            sp.dma_start(xt[:, t % 2], rows(x_src, t + 2)).then_inc(x_in_s[t % 2], 16)
                    sp.wait_ge(x_out[0], 16 * 5)
                    sp.wait_ge(x_out[1], 16 * 4)
                    sp.wait_ge(xn_out[0], 16 * 5)
                    sp.wait_ge(xn_out[1], 16 * 4)

                @block.tensor
                def _(pe):
                    n = 0
                    for b in range(NB):
                        if b >= 1:
                            pe.wait_ge(S["bc_ok"], b)
                        for c in range(DC):
                            pe.wait_ge(S["dg_ok"], n + 1)
                            nc.tensor.matmul(bank[:, c // 4, (c % 4) * P:(c % 4 + 1) * P], ones[:], dg[:, n % 2],
                                             start=True, stop=True).then_inc(S["bc_mm"], 1)
                            n += 1
                    pe.wait_ge(S["bc_ok"], NB)
                    pe.wait_ge(S["w_in"], 16)
                    pe.wait_ge(S["wr_in"], 16)

                    def turn_o(t):
                        pe.wait_ge(S["om_ok"], t + 1)
                        if t:
                            pe.wait_ge(S["oT_ok"], t)
                        for c in range(H):
                            last = nc.tensor.transpose(bank[:, 2 + c // 4, (c % 4) * P:(c % 4 + 1) * P],
                                                       om[:, c * P:(c + 1) * P], ident[:])
                        last.then_inc(S["oT_mm"], 1)

                    def product(t):
                        if t:
                            pe.wait_ge(S["tmp_ok"], t)
                        if attn:
                            pe.wait_ge(S["oT_ok"], t + 1)
                            for b in range(2):
                                for c in range(H):
                                    last = nc.tensor.matmul(bank[:, b, :], oT[:, t % 2, c], wo[:, c, b * 512:(b + 1) * 512],
                                                            start=(c == 0), stop=(c == H - 1))
                        else:
                            for g in range(4):
                                for c in range(2):
                                    last = nc.tensor.matmul(bank[:, g // 2, (g % 2) * GROUP:(g % 2 + 1) * GROUP],
                                                            pT[:, 2 * g + c, t], pw[:, g, c], start=(c == 0), stop=(c == 1))
                        last.then_inc(S["mm_done"], 1)

                    def turn_x(t):
                        pe.wait_ge(S["xn_ok"], t + 1)
                        if t:
                            pe.wait_ge(S["h2_ok"], t)
                        for c in range(DC):
                            last = nc.tensor.transpose(bank[:, 4 + c // 4, (c % 4) * P:(c % 4 + 1) * P],
                                                       xn[:, t % 2, c * P:(c + 1) * P], ident[:])
                        last.then_inc(S["xT_mm"], 1)

                    def router(t):
                        pe.wait_ge(S["h2_ok"], t + 1)
                        if t:
                            pe.wait_ge(S["lexp_ok"], t)
                        for c in range(DC):
                            last = nc.tensor.matmul(bank[:, 6, 0:E], h2[:, t % 2, c], wr[:, c], start=(c == 0), stop=(c == DC - 1))
                        last.then_inc(S["lg_mm"], 1)

                    def turn_aff(t):
                        pe.wait_ge(S["aff_ok"], t + 1)
                        if t:
                            pe.wait_ge(S["af_ok"], t)
                        nc.tensor.transpose(bank[0:E, 7, 0:P], sm[:, t % 2, 3], ident[:]).then_inc(S["affT_mm"], 1)

                    if attn:
                        turn_o(0)
                    for s in range(TT + 3):
                        if attn and s + 1 < TT:
                            turn_o(s + 1)
                        if s < TT:
                            product(s)
                        if 1 <= s <= TT:
                            turn_x(s - 1)
                        if 2 <= s <= TT + 1:
                            router(s - 2)
                        if s >= 3:
                            turn_aff(s - 3)
                    pe.wait_ge(S["top_mm"], 1)
                    nc.tensor.transpose(bank[:, 0, 0:E], vv[0:E], ident[0:E, 0:E])
                    nc.tensor.transpose(bank[:, 0, 32:32 + E], fi[0:E], ident[0:E, 0:E])
                    nc.tensor.transpose(bank[0:CAP_C, 0, 64:64 + E], vc[0:E], ident[0:E, 0:E])
                    nc.tensor.transpose(bank[0:CAP_C, 0, 96:96 + E], fc[0:E], ident[0:E, 0:E]).then_inc(S["top_mm"], 1)

                @block.gpsimd
                def _(pool):
                    k = 0
                    def root(dst, src, n, width, done):
                        nonlocal k
                        nc.gpsimd.tensor_scalar(src, src, 1.0 / width, EPS, ALU.mult, ALU.add).then_inc(S["pool_step"], 1)
                        k += 1
                        pool.wait_ge(S["pool_step"], k)
                        nc.gpsimd.tensor_tensor(dst, src, hpow[:, 0:n], ALU.pow).then_inc(done, 1)

                    def head_norm(t):
                        pool.wait_ge(S["oss_ok"], t + 1)
                        root(osm[:, t % 2, 1], osm[:, t % 2, 0], H, VD, S["orstd_ok"])

                    if attn:
                        head_norm(0)
                    for t in range(TT):
                        if attn and t + 1 < TT:
                            head_norm(t + 1)
                        pool.wait_ge(S["ssq_ok"], t + 1)
                        root(st1[:, t, 1:2], st1[:, t, 0:1], 1, D, S["rstd_ok"])

                @block.scalar
                def _(act):
                    for b in range(NB):
                        act.wait_ge(S["bc_mm"], DC * (b + 1))
                        dst = gA[:, b] if b < 2 else gB[:, b - 2]
                        nc.scalar.activation(dst.rearrange("p (b n) -> p b n", b=2), bank[:, 0:2, :], ACT.Copy
                                             ).then_inc(S["bc_ok"], 1)

                    def oT_out(t):
                        act.wait_ge(S["oT_mm"], t + 1)
                        if t >= 2:
                            act.wait_ge(S["mm_done"], t - 1)
                        nc.scalar.activation(oT[:, t % 2].rearrange("p (b c) n -> p b (c n)", b=2), bank[:, 2:4, :], ACT.Copy,
                                             scale=sub8[:]).then_inc(S["oT_ok"], 1)

                    if attn:
                        oT_out(0)
                    for s in range(TT + 2):
                        if attn and s + 1 < TT:
                            oT_out(s + 1)
                        if s < TT:
                            act.wait_ge(S["x_ok"], s + 1)
                            if s >= 2:
                                act.wait_ge(xn_out[s % 2], 16 * (s // 2))
                                act.wait_ge(S["xT_mm"], s - 1)
                            nc.scalar.activation(xn[:, s % 2], xt[:, s % 2], ACT.Square, accum_out=st1[:, s, 0:1]
                                                 ).then_inc(S["ssq_ok"], 1)
                            act.wait_ge(S["ssq_ok"], s + 1)
                            act.wait_ge(S["rstd_ok"], s + 1)
                            nc.scalar.activation(xn[:, s % 2], xt[:, s % 2], ACT.Copy, scale=st1[:, s, 1:2]
                                                 ).then_inc(S["xn_ok"], 1)
                        if s >= 2:
                            t = s - 2
                            act.wait_ge(S["lmax_ok"], t + 1)
                            nc.scalar.activation(sm[:, t % 2, 0], bank[:, 6, 0:E], ACT.Exp, bias=st1[:, t, 2:3],
                                                 accum_out=st1[:, t, 3:4]).then_inc(S["lexp_ok"], 1)

                @block.vector
                def _(dve):
                    step = Step(dve, S["dve_step"])
                    for cond in range(2):
                        step.count(nc.vector.scalar_tensor_tensor(
                            gains[:, g2, :, cond], modc[:, base + SCALE2 * DC:base + SCALE2 * DC + DC, cond], 1.0,
                            colsA[:, 112 + layer * DC:112 + layer * DC + DC], ALU.add, ALU.mult))
                    if not attn:
                        for cond in range(2):
                            gate = modc[:, base + GATE1 * DC:base + GATE1 * DC + DC, cond]
                            step.link(nc.vector.tensor_tensor(pcol[:, 0, :, cond], gate, colsB[:, 24:32], ALU.mult))
                            step.link(nc.vector.tensor_tensor(pcol[:, 1, :, cond], pcol[:, 0, :, cond], colsB[:, 16:24], ALU.mult))
                    n = 0
                    for b in range(NB):
                        for c in range(DC):
                            if n >= 2:
                                dve.wait_ge(S["bc_mm"], n - 1)
                            col = (modc[:, base + GATE1 * DC + c, b:b + 1] if attn
                                   else pcol[:, b // 2, c, b % 2:b % 2 + 1])
                            nc.vector.tensor_scalar(dg[:, n % 2], ident[:], col, None, ALU.mult).then_inc(S["dg_ok"], 1)
                            n += 1

                    def head_norm(t):
                        if t:
                            dve.wait_ge(S["oT_mm"], t)
                        o = oraw[:, t].rearrange("p (h d) -> p h d", h=H)
                        m = om[:].rearrange("p (h d) -> p h d", h=H)
                        step.link(nc.vector.tensor_tensor(om[:], oraw[:, t], oraw[:, t], ALU.mult))
                        nc.vector.tensor_reduce(osm[:, t % 2, 0], m, AX.X, ALU.add).then_inc(S["oss_ok"], 1)
                        dve.wait_ge(S["orstd_ok"], t + 1)
                        dve.wait_ge(S["oss_ok"], t + 1)
                        nc.vector.tensor_tensor(m, o, osm[:, t % 2, 1].unsqueeze(2).to_broadcast([P, H, VD]), ALU.mult
                                                ).then_inc(S["om_ok"], 1)

                    if attn:
                        head_norm(0)
                    for s in range(TT + 3):
                        if attn and s + 1 < TT:
                            head_norm(s + 1)
                        if s < TT:
                            cond = cond_of[s]
                            dve.wait_ge(S["mm_done"], s + 1)
                            dve.wait_ge(S["bc_ok"], NB)
                            dve.wait_ge(x_in_s[s % 2], 16 * (s // 2 + 1))
                            y = bank[:, 0:2, :]
                            nc.vector.tensor_tensor(y, y, gA[:, cond].rearrange("p (b n) -> p b n", b=2), ALU.mult
                                                    ).then_inc(S["xu"], 1)
                            if not attn:
                                step.link(nc.vector.tensor_tensor(xt[:, s % 2], xt[:, s % 2], gB[:, cond], ALU.add))
                            dve.wait_ge(S["xu"], s + 1)
                            xv = xt[:, s % 2].rearrange("p (b n) -> p b n", b=2)
                            nc.vector.tensor_tensor(xv, xv, y, ALU.add).then_inc(S["x_ok"], 1)
                            dve.wait_ge(S["x_ok"], s + 1)
                            nc.vector.memset(st1[:, s, 4:5], 0.0).then_inc(S["tmp_ok"], 1)
                        if 1 <= s <= TT:
                            t = s - 1
                            dve.wait_ge(S["xT_mm"], t + 1)
                            if t >= 2:
                                dve.wait_ge(S["lg_mm"], t - 1)
                            cond = cond_of[t]
                            dve.wait_ge(S["dve_step"], 2)
                            for c in range(DC):
                                last = nc.vector.tensor_scalar(
                                    h2[:, t % 2, c], bank[:, 4 + c // 4, (c % 4) * P:(c % 4 + 1) * P],
                                    gains[:, g2, c, cond:cond + 1], modc[:, base + SHIFT2 * DC + c, cond:cond + 1],
                                    ALU.mult, ALU.add)
                            last.then_inc(S["h2_ok"], 1)
                        if 2 <= s <= TT + 1:
                            t = s - 2
                            dve.wait_ge(S["lg_mm"], t + 1)
                            nc.vector.tensor_reduce(st1[:, t, 2:3], bank[:, 6, 0:E], AX.X, ALU.max, negate=True
                                                    ).then_inc(S["lmax_ok"], 1)
                            dve.wait_ge(S["lexp_ok"], t + 1)
                            step.link(nc.vector.reciprocal(st1[:, t, 5:6], st1[:, t, 3:4]))
                            if t >= 2:
                                dve.wait_ge(S["affT_mm"], t - 1)
                            nc.vector.tensor_scalar(sm[:, t % 2, 3], sm[:, t % 2, 0], st1[:, t, 5:6], None, ALU.mult
                                                    ).then_inc(S["aff_ok"], 1)
                        if s >= 3:
                            t = s - 3
                            dve.wait_ge(S["affT_mm"], t + 1)
                            nc.vector.tensor_copy(af[0:E, t * P:(t + 1) * P], bank[0:E, 7, 0:P]).then_inc(S["af_ok"], 1)
                    dve.wait_ge(S["af_ok"], TT)
                    for vals, idx, lo, n, cap in ((vv, ii, 0, N_LAT, CAP_L), (vc, ic, N_LAT, N_CTX, CAP_C)):
                        work = af[0:E, lo:lo + n]
                        for r in range(cap // 8):
                            v8 = vals[0:E, 8 * r:8 * r + 8]
                            step.link(nc.vector.max(v8, work))
                            step.link(nc.vector.max_index(idx[0:E, 8 * r:8 * r + 8], v8, work))
                            step.link(nc.vector.match_replace(work, v8, work, -1.0))
                    step.link(nc.vector.tensor_copy(fi[0:E], ii[0:E]))
                    step.wait()
                    nc.vector.tensor_copy(fc[0:E], ic[0:E]).then_inc(S["top_mm"], 1)
                    dve.wait_ge(S["top_mm"], 2)
                    for dst, lo, parts in ((valL, 0, P), (idxL, 32, P), (valC, 64, CAP_C), (idxC, 96, CAP_C)):
                        nc.vector.tensor_copy(dst[0:parts, 0:E], bank[0:parts, 0, lo:lo + E])
                        nc.vector.tensor_copy(dst[0:parts, E:E + 1], bank[0:parts, 0, lo:lo + 1])

        def experts(layer):
            g2 = 2 * layer + 1
            base = layer * SECT
            with Stage() as st:
                off = exp_at
                xe, off = sb(f"ex_xe{layer}", [P, D], off)
                xeC, off = sb(f"ex_xeC{layer}", [P, D], off)
                xT, off = sb(f"ex_xT{layer}", [P, DC, CAP], off)
                hid, off = sb(f"ex_hid{layer}", [P, FF // P, CAP], off)
                ge, off = sb(f"ex_ge{layer}", [P, 2, 3 * CAP], off)
                t1, off = sb(f"ex_t1{layer}", [P, 3 * CAP], off)
                t2, off = sb(f"ex_t2{layer}", [P, 3 * CAP], off)
                yT, off = sb(f"ex_yT{layer}", [P, DC, CAP], off)
                ye, off = sb(f"ex_ye{layer}", [P, D], off)
                yeC, off = sb(f"ex_yeC{layer}", [P, D], off)
                gi, off = sb(f"ex_gi{layer}", [P, 2], off, U32)
                si, off = sb(f"ex_si{layer}", [P, 2], off, U32)
                assert off <= nc.sbuf_usable_end, off
                S = {}
                for n in ("xe_in xeT_mm xT_ok gate_mm up_mm exp_ok hid_step hid_ok y_mm yT_ok yT_mm ye_ok yeC_ok ye_read yeC_read ye_free gidx0_ok gidx_ok "
                          "sidx_ok xe_free").split():
                    S[n] = sem(st, f"ex{layer}_" + n)
                scat = sem(st, f"ex{layer}_scattered")
                block = st.enter_context(nc.Block())
                NJ = len(PIECES)
                r0 = 16 * E * layer
                GB, UB, YB, TB = (0, 1), (2, 3), (4, 5, 6), 7

                @block.sync
                def _(sp):
                    for i in range(RING_EARLY, 12):
                        dst, src = ring_source(layer, 0, i)
                        sp.dma_start(dst, src).then_inc(ring_in[i], 16)
                    with sp.Fori(1, E) as e:
                        for j in range(NJ):
                            sp.wait_ge(S["up_mm"], NJ * e - NJ + j + 1)
                            for i in (2 * j, 2 * j + 1):
                                dst, src = ring_source(layer, e, i)
                                sp.dma_start(dst, src).then_inc(ring_in[i], 16)
                        sp.wait_ge(S["y_mm"], 3 * e + 1)
                        for i in range(8, 12):
                            dst, src = ring_source(layer, e, i)
                            sp.dma_start(dst, src).then_inc(ring_in[i], 16)

                @block.gpsimd
                def _(pool):
                    def gather(e, copied, count):
                        nc.gpsimd.tensor_copy(gi[:, 0:1], idxL[:, bass.ds(e, 1)])
                        nc.gpsimd.tensor_copy(gi[0:CAP_C, 1:2], idxC[0:CAP_C, bass.ds(e, 1)]).then_inc(copied, 1)
                        pool.wait_ge(S["gidx0_ok"], 1)
                        pool.wait_ge(copied, count)
                        nc.gpsimd.indirect_dma_start(out=xe[:], out_offset=None, in_=xnrm[0],
                                                     in_offset=bass.IndirectOffsetOnAxis(ap=gi[:, 0:1], axis=0)
                                                     ).then_inc(S["xe_in"], 16)
                        nc.gpsimd.indirect_dma_start(out=xeC[0:CAP_C], out_offset=None, in_=xnrm[1],
                                                     in_offset=bass.IndirectOffsetOnAxis(ap=gi[0:CAP_C, 1:2], axis=0)
                                                     ).then_inc(S["xe_in"], 16)

                    for n in ("ye_free", "ye_read", "yeC_read"):
                        pool.sem_inc(S[n], 1)
                    gather(0, S["gidx0_ok"], 1)
                    with pool.Fori(0, E) as e:
                        pool.wait_ge(S["xeT_mm"], 3 * e + 3)
                        pool.wait_ge(S["xe_in"], 32 * e + 32)
                        gather(e + 1, S["gidx_ok"], e + 1)
                        nc.gpsimd.tensor_copy(si[:, 0:1], idxL[:, bass.ds(e, 1)])
                        nc.gpsimd.tensor_copy(si[0:CAP_C, 1:2], idxC[0:CAP_C, bass.ds(e, 1)]).then_inc(S["sidx_ok"], 1)
                        pool.wait_ge(S["ye_ok"], 1)
                        pool.wait_ge(S["sidx_ok"], e + 1)
                        pool.wait_ge(S["ye_ok"], e + 1)
                        nc.gpsimd.indirect_dma_start(out=xres[0], out_offset=bass.IndirectOffsetOnAxis(ap=si[:, 0:1], axis=0),
                                                     in_=ye[:], in_offset=None, compute_op=ALU.add).then_inc(scat, 16)
                        pool.sem_inc(S["ye_read"], 1)
                        pool.wait_ge(S["yeC_ok"], 1)
                        pool.wait_ge(S["yeC_ok"], e + 1)
                        nc.gpsimd.indirect_dma_start(out=xres[1], out_offset=bass.IndirectOffsetOnAxis(ap=si[0:CAP_C, 1:2], axis=0),
                                                     in_=yeC[0:CAP_C], in_offset=None, compute_op=ALU.add).then_inc(scat, 16)
                        pool.sem_inc(S["yeC_read"], 1)
                        pool.wait_ge(scat, 32 * e + 32)
                        pool.sem_inc(S["ye_free"], 1)
                    pool.wait_ge(S["xe_in"], 32 * E + 32)
                    pool.wait_ge(scat, 32 * E)

                @block.tensor
                def _(pe):
                    def turn_x(n, first=False):
                        pe.wait_ge(S["xe_in"], 32 * n + 32)
                        if not first:
                            pe.wait_ge(S["yeC_read"], n)
                        for b, c0 in ((YB[2], 0), (TB, 4)):
                            for c in range(c0, c0 + 4):
                                last = nc.tensor.transpose(bank[:, b, (c - c0) * P:(c - c0 + 1) * P], xe[:, c * P:(c + 1) * P], ident[:])
                            last.then_inc(S["xeT_mm"], 1)
                        for c in range(DC):
                            last = nc.tensor.transpose(bank[:, YB[1], c * CAP_C:(c + 1) * CAP_C], xeC[0:CAP_C, c * P:(c + 1) * P],
                                                       ident[0:CAP_C, 0:CAP_C])
                        last.then_inc(S["xeT_mm"], 1)

                    pe.sem_inc(S["y_mm"], 1)
                    pe.sem_inc(S["yT_mm"], 1)
                    turn_x(0, first=True)
                    with pe.Fori(0, E) as e:
                        pe.wait_ge(S["xT_ok"], 3 * e + 3)
                        for j, nf in enumerate(PIECES):
                            pe.wait_ge(S["hid_ok"], NJ * e + j + 1)
                            if j == 1:
                                pe.wait_ge(S["ye_read"], e + 1)
                            for banks, i, done in ((GB, 2 * j, "gate_mm"), (UB, 2 * j + 1, "up_mm")):
                                pe.wait_ge(ring_in[i], r0 + 16 * e + 16)
                                wv = ring[i][:, 0:DC * nf * P].rearrange("p (c f) -> p c f", c=DC)
                                for f in range(nf):
                                    for c in range(DC):
                                        last = nc.tensor.matmul(bank[:, banks[j % 2], f * CAP:(f + 1) * CAP],
                                                                wv[:, c, f * P:(f + 1) * P], xT[:, c],
                                                                start=(c == 0), stop=(c == DC - 1))
                                last.then_inc(S[done], 1)
                        turn_x(e + 1)
                        for m in range(DC):
                            if m == 0:
                                pass
                            if m == 3:
                                pe.wait_ge(S["xT_ok"], 3 * e + 6)
                            f = 0
                            for j, nf in enumerate(PIECES):
                                if m == 0:
                                    pe.wait_ge(S["hid_ok"], NJ * e + j + 3)
                                    pe.wait_ge(ring_in[8 + j], r0 + 16 * e + 16)
                                wv = ring[8 + j][:, 0:nf * D].rearrange("p (q d) -> p q d", q=nf)
                                for q in range(nf):
                                    last = nc.tensor.matmul(bank[:, YB[m // 3], (m % 3) * CAP:(m % 3 + 1) * CAP],
                                                            wv[:, q, m * P:(m + 1) * P], hid[:, f],
                                                            start=(f == 0), stop=(f == FF // P - 1))
                                    f += 1
                            if m in (2, 5, 7):
                                last.then_inc(S["y_mm"], 1)
                        for m in range(DC):
                            pe.wait_ge(S["yT_ok"], DC * e + m + 1)
                            last = nc.tensor.transpose(bank[:, (GB[1], UB[1])[m // 4], (m % 4) * P:(m % 4 + 1) * P],
                                                       yT[:, m, 0:P], ident[:])
                        last.then_inc(S["yT_mm"], 1)
                        for m in range(DC):
                            last = nc.tensor.transpose(bank[0:CAP_C, (TB, YB[0])[m // 4], (m % 4) * P:(m % 4 + 1) * P],
                                                       yT[:, m, P:CAP], ident[:])
                        last.then_inc(S["yT_mm"], 1)

                @block.scalar
                def _(act):
                    with act.Fori(0, E) as e:
                        for j, nf in enumerate(PIECES):
                            act.wait_ge(S["gate_mm"], NJ * e + j + 1)
                            act.wait_ge(S["hid_ok"], NJ * e + j + 1)
                            nc.scalar.activation(ge[:, j % 2, 0:nf * CAP], bank[:, GB[j % 2], 0:nf * CAP], ACT.Exp, scale=-1.0
                                                 ).then_inc(S["exp_ok"], 1)
                        act.wait_ge(S["yT_mm"], 2 * e + 1)
                        for m in range(DC):
                            if m % 3 == 0:
                                act.wait_ge(S["y_mm"], 3 * e + m // 3 + 2)
                            src = bank[:, YB[m // 3], (m % 3) * CAP:(m % 3 + 1) * CAP]
                            gate = modc[:, base + GATE2 * DC + m]
                            nc.scalar.activation(yT[:, m, 0:P], src[:, 0:P], ACT.Copy, scale=gate[:, 0:1])
                            nc.scalar.activation(yT[:, m, P:CAP], src[:, P:CAP], ACT.Copy, scale=gate[:, 1:2]
                                                 ).then_inc(S["yT_ok"], 1)
                        act.wait_ge(S["yT_mm"], 2 * e + 2)
                        act.wait_ge(S["ye_free"], e + 1)
                        for i, b in enumerate((GB[1], UB[1])):
                            last = nc.scalar.activation(ye[:, i * 512:(i + 1) * 512], bank[:, b], ACT.Copy,
                                                        scale=valL[:, bass.ds(e, 1)])
                        last.then_inc(S["ye_ok"], 1)

                @block.vector
                def _(dve):
                    nc.vector.memset(t1[:, 0:8], 0.0).then_inc(S["hid_ok"], 1)
                    nc.vector.memset(t2[:, 0:8], 0.0).then_inc(S["hid_ok"], 1)
                    dve.wait_ge(S["hid_ok"], 2)

                    def adaln(n):
                        for b, c0 in ((YB[2], 0), (TB, 4)):
                            dve.wait_ge(S["xeT_mm"], 3 * n + 1 + c0 // 4)
                            for c in range(c0, c0 + 4):
                                last = nc.vector.tensor_scalar(xT[:, c, 0:P], bank[:, b, (c - c0) * P:(c - c0 + 1) * P],
                                                               gains[:, g2, c, 0:1], modc[:, base + SHIFT2 * DC + c, 0:1],
                                                               ALU.mult, ALU.add)
                            last.then_inc(S["xT_ok"], 1)
                        dve.wait_ge(S["xeT_mm"], 3 * n + 3)
                        for c in range(DC):
                            last = nc.vector.tensor_scalar(xT[:, c, P:CAP], bank[:, YB[1], c * CAP_C:(c + 1) * CAP_C],
                                                           gains[:, g2, c, 1:2], modc[:, base + SHIFT2 * DC + c, 1:2],
                                                           ALU.mult, ALU.add)
                        last.then_inc(S["xT_ok"], 1)

                    adaln(0)
                    with dve.Fori(0, E) as e:
                        for j, nf in enumerate(PIECES):
                            n = nf * CAP
                            step = Step(dve, S["hid_step"], 3 * NJ * e + 3 * j)
                            dve.wait_ge(S["exp_ok"], NJ * e + j + 1)
                            dve.wait_ge(S["hid_ok"], NJ * e + j + 2)
                            step.link(nc.vector.tensor_scalar(t1[:, 0:n], ge[:, j % 2, 0:n], 1.0, None, ALU.add))
                            step.link(nc.vector.reciprocal(t2[:, 0:n], t1[:, 0:n]))
                            step.link(nc.vector.tensor_tensor(t1[:, 0:n], bank[:, GB[j % 2], 0:n], t2[:, 0:n], ALU.mult))
                            dve.wait_ge(S["up_mm"], NJ * e + j + 1)
                            if j == 0:
                                dve.wait_ge(S["y_mm"], 3 * e + 1)
                            nc.vector.tensor_tensor(hid[:, PIECE0[j]:PIECE0[j] + nf].rearrange("p f s -> p (f s)"), t1[:, 0:n],
                                                    bank[:, UB[j % 2], 0:n], ALU.mult).then_inc(S["hid_ok"], 1)
                        adaln(e + 1)
                        dve.wait_ge(S["yT_mm"], 2 * e + 3)
                        dve.wait_ge(S["ye_free"], e + 1)
                        for i, b in enumerate((TB, YB[0])):
                            last = nc.vector.tensor_scalar(yeC[0:CAP_C, i * 512:(i + 1) * 512], bank[0:CAP_C, b],
                                                           valC[0:CAP_C, bass.ds(e, 1)], None, ALU.mult)
                        last.then_inc(S["yeC_ok"], 1)

        PAD = 8
        SPANS = ((0, N_LAT, 0), (N_LAT, N_CTX, 1))
        WL = N_LAT + 2 * PAD
        WIDE = WL + N_CTX + 2 * PAD

        def pool_mixer(hw, off):
            with Stage() as st:
                xt, off = sb("pm_xt", [P, 4, D], off)
                s1, off = sb("pm_s1", [P, 2, WIDE], off)
                inv, off = sb("pm_inv", [P, 4, N_TOK], off)
                sq, off = sb("pm_sq", [P, D], off)
                st1, off = sb("pm_st", [P, TT, 2], off)
                assert off <= nc.sbuf_usable_end, off
                S = {}
                for n in "inv_in ssq_ok rstd_ok xn_ok xT_mm h_ok step pool_step zero_ok gain_ok".split():
                    S[n] = sem(st, "pm_" + n)
                x_s = [sem(st, f"pm_x_in{i}") for i in range(4)]
                block = st.enter_context(nc.Block())

                def place_of(t):
                    return PAD + t * P if t < LT else WL + PAD

                @block.sync
                def _(sp):
                    for t in range(TT):
                        if t >= 4:
                            sp.wait_ge(S["xT_mm"], t - 3)
                        sp.dma_start(xt[:, t % 4], rows(xres, t)).then_inc(x_s[t % 4], 16)
                        if t == 3:
                            sp.dma_start(inv[:].rearrange("p g n -> p (g n)"), a["inv_count"].rearrange("g n -> (g n)").partition_broadcast(P)
                                         ).then_inc(S["inv_in"], 16)

                @block.gpsimd
                def _(pool):
                    for i, (lo, n) in enumerate(((0, PAD), (PAD + N_LAT, 2 * PAD), (WIDE - PAD, PAD))):
                        nc.gpsimd.memset(hw[:, :, lo:lo + n], 0.0).then_inc(S["zero_ok"], 1)
                    nc.gpsimd.memset(s1[:], 0.0).then_inc(S["zero_ok"], 1)
                    for t in range(TT):
                        pool.wait_ge(S["ssq_ok"], t + 1)
                        nc.gpsimd.tensor_scalar(st1[:, t, 0:1], st1[:, t, 0:1], 1.0 / D, EPS, ALU.mult, ALU.add
                                                ).then_inc(S["pool_step"], 1)
                        pool.wait_ge(S["pool_step"], t + 1)
                        nc.gpsimd.tensor_tensor(st1[:, t, 1:2], st1[:, t, 0:1], hpow[:, 0:1], ALU.pow).then_inc(S["rstd_ok"], 1)

                @block.scalar
                def _(act):
                    for t in range(TT):
                        act.wait_ge(x_s[t % 4], 16 * (t // 4 + 1))
                        if t:
                            act.wait_ge(S["ssq_ok"], t)
                        nc.scalar.activation(sq[:], xt[:, t % 4], ACT.Square, accum_out=st1[:, t, 0:1]).then_inc(S["ssq_ok"], 1)
                        act.wait_ge(S["rstd_ok"], t + 1)
                        nc.scalar.activation(xt[:, t % 4], xt[:, t % 4], ACT.Copy, scale=st1[:, t, 1:2]).then_inc(S["xn_ok"], 1)

                @block.tensor
                def _(pe):
                    for t in range(TT):
                        pe.wait_ge(S["xn_ok"], t + 1)
                        if t >= 4:
                            pe.wait_ge(S["h_ok"], t - 3)
                        for c in range(DC):
                            last = nc.tensor.transpose(bank[:, 2 * (t % 4) + c // 4, (c % 4) * P:(c % 4 + 1) * P],
                                                       xt[:, t % 4, c * P:(c + 1) * P], ident[:])
                        last.then_inc(S["xT_mm"], 1)

                @block.vector
                def _(dve):
                    step = Step(dve, S["step"])
                    for cond in range(2):
                        last = nc.vector.scalar_tensor_tensor(gains[:, 2, :, cond], modc[:, SECT + SCALE1 * DC:SECT + SCALE1 * DC + DC, cond],
                                                              1.0, colsA[:, 96 + DC:96 + 2 * DC], ALU.add, ALU.mult)
                    step.link(last)
                    for t in range(TT):
                        dve.wait_ge(S["xT_mm"], t + 1)
                        cond = 0 if t < LT else 1
                        for c in range(DC):
                            last = nc.vector.tensor_scalar(hw[:, c, place_of(t):place_of(t) + P],
                                                           bank[:, 2 * (t % 4) + c // 4, (c % 4) * P:(c % 4 + 1) * P],
                                                           gains[:, 2, c, cond:cond + 1],
                                                           modc[:, SECT + SHIFT1 * DC + c, cond:cond + 1], ALU.mult, ALU.add)
                        last.then_inc(S["h_ok"], 1)
                    dve.wait_ge(S["h_ok"], TT)
                    dve.wait_ge(S["zero_ok"], 4)
                    dve.wait_ge(S["inv_in"], 16)
                    for c in range(DC):
                        g = c * P // GROUP
                        src = hw[:, c]
                        half = 0
                        for k in range(g + 1):
                            dst = s1[:, k % 2]
                            back = 1 if half == 0 else half
                            fwd = half
                            lo, hi = back, WIDE - fwd
                            step.link(nc.vector.tensor_tensor(dst[:, lo:hi], src[:, lo - back:hi - back], src[:, lo + fwd:hi + fwd], ALU.add))
                            src, half = dst, (1 if half == 0 else 2 * half)
                        for lo, n, cond in SPANS:
                            p0 = PAD if cond == 0 else WL + PAD
                            step.link(nc.vector.tensor_tensor(src[:, p0:p0 + n], src[:, p0:p0 + n], inv[:, g, lo:lo + n], ALU.mult))
                            step.link(nc.vector.tensor_tensor(hw[:, c, p0:p0 + n], src[:, p0:p0 + n], hw[:, c, p0:p0 + n], ALU.subtract))

        def final_norm():
            off = persistent_end
            with Stage() as st:
                xt, off = sb("fn_xt", [P, TT, D], off)
                yt, off = sb("fn_yt", [P, TT, D], off)
                fg, off = sb("fn_fg", [P, D], off)
                sq, off = sb("fn_sq", [P, D], off)
                st1, off = sb("fn_st", [P, TT, 2], off)
                S = {n: sem(st, "fn_" + n) for n in "fg_in ssq_ok rstd_ok y_ok out_ok pool_step".split()}
                x_s = [sem(st, f"fn_x_in{t}") for t in range(TT)]
                block = st.enter_context(nc.Block())
                y_out = [out["y_sample"][0], out["y_prompt"][0]]

                @block.sync
                def _(sp):
                    for t in range(TT):
                        sp.dma_start(xt[:, t], rows(xres, t)).then_inc(x_s[t], 16)
                        if t == 0:
                            sp.dma_start(fg[:], a["final_g"].partition_broadcast(P)).then_inc(S["fg_in"], 16)
                    for t in range(TT):
                        sp.wait_ge(S["y_ok"], t + 1)
                        sp.dma_start(rows(y_out, t), yt[:, t]).then_inc(S["out_ok"], 16)
                    sp.wait_ge(S["out_ok"], 16 * TT)

                @block.scalar
                def _(act):
                    for t in range(TT):
                        act.wait_ge(x_s[t], 16)
                        if t:
                            act.wait_ge(S["ssq_ok"], t)
                        nc.scalar.activation(sq[:], xt[:, t], ACT.Square, accum_out=st1[:, t, 0:1]).then_inc(S["ssq_ok"], 1)

                @block.gpsimd
                def _(pool):
                    for t in range(TT):
                        pool.wait_ge(S["ssq_ok"], t + 1)
                        nc.gpsimd.tensor_scalar(st1[:, t, 0:1], st1[:, t, 0:1], 1.0 / D, EPS, ALU.mult, ALU.add
                                                ).then_inc(S["pool_step"], 1)
                        pool.wait_ge(S["pool_step"], t + 1)
                        nc.gpsimd.tensor_tensor(st1[:, t, 1:2], st1[:, t, 0:1], hpow[:, 0:1], ALU.pow).then_inc(S["rstd_ok"], 1)

                @block.vector
                def _(dve):
                    dve.wait_ge(S["fg_in"], 16)
                    for t in range(TT):
                        dve.wait_ge(S["rstd_ok"], t + 1)
                        nc.vector.scalar_tensor_tensor(yt[:, t], xt[:, t], st1[:, t, 1:2], fg[:], ALU.mult, ALU.mult
                                                       ).then_inc(S["y_ok"], 1)

        hT = nc.alloc_sbuf_tensor_at("hT", [P, DC, N_TOK], F32, offset=big_at)
        setup_and_norm(hT)
        oraw_at = nc.sbuf_usable_end // 32 * 32 - 4 * TT * D
        oraw = nc.alloc_sbuf_tensor_at("oraw", [P, TT, D], F32, offset=oraw_at)
        attention(hT, oraw, persistent_end + 4 * DC * N_TOK)
        mixer_and_route(0, oraw, None, late_at)
        experts(0)
        hw = nc.alloc_sbuf_tensor_at("hw", [P, DC, WIDE], F32, offset=big_at)
        pool_mixer(hw, ring_at)
        class Tiles:
            def __getitem__(self, key):
                _, c, t = key
                p0 = PAD + t * P if t < LT else WL + PAD
                return hw[:, c, p0:p0 + P]
        mixer_and_route(1, None, Tiles(), late_at)
        experts(1)
        final_norm()


_INS = ['x_prompt', 'x_sample', 'cache_k', 'cache_v', 'c', 'c_ctx', 'w_mod', 'b_mod', 'norm1_g', 'norm2_g',
        'attn_wqkv', 'attn_wo', 'lambda_q1', 'lambda_k1', 'lambda_q2', 'lambda_k2', 'subln_g', 'pool_w', 'pool_b',
        'pool_scale', 'router_w', 'expert_w_gate', 'expert_w_up', 'expert_w_down', 'final_g']
_OUTS = [('y_prompt', (1, 128, 1024)), ('y_sample', (1, 1024, 1024)), ('new_cache_k', (1, 1, 128, 8, 128)),
         ('new_cache_v', (1, 1, 128, 8, 128))]


def kernel(**inputs):
    import concourse.bacc as _bacc
    from concourse.bass_utils import run_bass_kernel_spmd as _run

    nc = _bacc.Bacc("TRN2", target_bir_lowering=False, num_devices=1)
    arrays, a, out = {}, {}, {}
    cos, sin = rope_tables()
    constants = {"rope_cos": cos, "rope_sin": sin, "inv_count": window_counts(), "ident": np.eye(P, dtype=np.float32)}
    for name, x in [*((n, inputs[n]) for n in _INS), *constants.items()]:
        x = np.ascontiguousarray(x)
        arrays[f"in_{name}"] = x
        a[name] = nc.dram_tensor(f"in_{name}", x.shape, mybir.dt.from_np(x.dtype), kind="ExternalInput").ap()
    for name, shape in _OUTS:
        out[name] = nc.dram_tensor(f"out_{name}", shape, F32, kind="ExternalOutput").ap()
    build(nc, a, out)
    r = _run(nc, [arrays], core_ids=[0])
    return tuple(r.results[0][f"out_{name}"] for name, _ in _OUTS)
```

```python
from contextlib import ExitStack

import numpy as np

import concourse.bass as bass
from concourse import mybir

F32 = mybir.dt.float32
F32R = mybir.dt.float32r
U32 = mybir.dt.uint32
ALU = mybir.AluOpType
ACT = mybir.ActivationFunctionType
AX = mybir.AxisListType

P = 128
D = 1024
DC = D // P
N_LAT = 1024
N_CTX = 128
LT = N_LAT // P
TT = LT + N_CTX // P
N_TOK = N_LAT + N_CTX
LAYERS = 2
H = 8
HD = 64
VD = 2 * HD
PAST = 128
KEYS = N_LAT + PAST
GRID_W = 64
ROPE_BASE = 10000.0
WINDOWS = (2, 4, 8, 16)
GROUP = D // len(WINDOWS)
EDGE = max(WINDOWS) // 2
E = 16
FF = 1408
CAP_L = 2 * N_LAT // E
CAP_C = 2 * N_CTX // E
CAP = CAP_L + CAP_C
EPS = 1e-6
LAM_INIT = 0.2
BANK = 512

PIECES = [3, 3, 3, 2]
PIECE0 = [0, 3, 6, 9]
SLOT = 3 * P * DC
RING_EARLY = (5, 6)

SHIFT1, SCALE1, GATE1, SHIFT2, SCALE2, GATE2 = range(6)
SECT = 6 * DC


class Step:

    def __init__(self, eng, sem, start=0):
        self.eng, self.sem, self.start, self.n = eng, sem, start, 0

    def count(self, ins):
        ins.then_inc(self.sem, 1)
        self.n += 1

    def wait(self):
        self.eng.wait_ge(self.sem, self.start + self.n)

    def link(self, ins):
        self.count(ins)
        self.wait()


def rope_tables():
    t = np.arange(N_LAT)
    half = HD // 2
    inv = (np.float32(ROPE_BASE) ** (-np.arange(0, half, 2, dtype=np.float32) / np.float32(half))).astype(np.float32)
    row = (t // GRID_W).astype(np.float32)[:, None] * inv
    col = (t % GRID_W).astype(np.float32)[:, None] * inv
    cos = np.concatenate([np.cos(row), np.cos(row), np.cos(col), np.cos(col)], axis=1)
    sin = np.concatenate([-np.sin(row), np.sin(row), -np.sin(col), np.sin(col)], axis=1)
    both = lambda m: np.concatenate([m, m], axis=1).astype(np.float32)
    return both(cos), both(sin)


def window_edges():
    out = np.zeros((len(WINDOWS), 2, 2, EDGE), np.float32)
    for g, w in enumerate(WINDOWS):
        for i, n in enumerate((N_LAT, N_CTX)):
            t = np.arange(n)
            full = (w / (np.clip(t + w // 2, 0, n) - np.clip(t - w // 2, 0, n))).astype(np.float32)
            out[g, i, 0], out[g, i, 1] = full[:EDGE], full[-EDGE:]
    return out


def build(nc, a, out):
    with ExitStack() as ctx:
        place = {}

        def sb(name, shape, offset, dtype=F32):
            t = nc.alloc_sbuf_tensor_at(name, list(shape), dtype, offset=offset)
            size = 4 * int(np.prod(shape[1:]))
            return t, (offset + size + 31) // 32 * 32

        def sem(scope, name):
            s = nc.alloc_semaphore(name)
            scope.sems.append(s)
            return s

        class Stage(ExitStack):
            def __init__(self):
                super().__init__()
                self.sems = []
                self.callback(self.clear)

            def clear(self):
                nc.clear_and_free_semaphores(self.sems)
                nc.all_engine_barrier()

        bank = ctx.enter_context(nc.psum_tensor("bank", [P, 8, BANK], F32))

        at = 16512
        ident, at = sb("ident", [P, P], at)
        ones, at = sb("ones", [P, P], at)
        colsA, at = sb("colsA", [P, 128], at)
        colsB, at = sb("colsB", [P, 40], at)
        bmod2, at = sb("bmod2", [P, LAYERS * SECT, 2], at)
        modc, at = sb("modc", [P, LAYERS * SECT, 2], at)
        gains, at = sb("gains", [P, 4, DC, 2], at)
        silu, at = sb("silu", [P, 2, DC], at)
        nlam, at = sb("nlam", [P, 1], at)
        sub8, at = sb("sub8", [P, 1], at)
        hpow, at = sb("hpow", [P, 16], at)
        valL, at = sb("valL", [P, E + 1], at)
        valC, at = sb("valC", [P, E + 1], at)
        idxL, at = sb("idxL", [P, E + 1], at, U32)
        idxC, at = sb("idxC", [P, E + 1], at, U32)
        persistent_end = at

        xres = [nc.dram_tensor("xres_lat", (N_LAT, D), F32, kind="Internal").ap(),
                nc.dram_tensor("xres_ctx", (N_CTX, D), F32, kind="Internal").ap()]
        xnrm = [nc.dram_tensor("xnrm_lat", (N_LAT, D), F32, kind="Internal").ap(),
                nc.dram_tensor("xnrm_ctx", (N_CTX, D), F32, kind="Internal").ap()]

        oscr = [nc.dram_tensor("heads_lat", (N_LAT, D), F32, kind="Internal").ap(),
                nc.dram_tensor("heads_ctx", (N_CTX, D), F32, kind="Internal").ap()]

        def rows(pair, t):
            return pair[0][t * P:(t + 1) * P, :] if t < LT else pair[1][:, :]

        x_in = [a["x_sample"][0], a["x_prompt"][0]]

        big_at = persistent_end
        BIG = 4 * DC * (N_TOK + 32)
        ring_at = big_at + BIG
        SB = 4 * SLOT
        slot_off = [ring_at + i * SB for i in range(6)]
        late_at = ring_at + 6 * SB
        slot_off += [big_at + i * SB for i in range(3)]
        slot_off += [late_at + i * SB for i in range(3)]
        assert 3 * SB <= BIG
        exp_at = late_at + 3 * SB
        ring = [nc.alloc_sbuf_tensor_at(f"ring{i}", [P, SLOT], F32, offset=slot_off[i]) for i in range(12)]
        ring_in = [ctx.enter_context(nc.semaphore(f"ring_in{i}")) for i in range(12)]

        def ring_source(layer, e, i):
            j = i // 2 if i < 8 else i - 8
            nf, f0 = PIECES[j] * P, PIECE0[j] * P
            if i < 8:
                w = a["expert_w_gate" if i % 2 == 0 else "expert_w_up"]
                src = w[layer, e].rearrange("(c p) f -> p c f", p=P)[:, :, f0:f0 + nf]
                return ring[i][:, 0:DC * nf].rearrange("p (c f) -> p c f", c=DC), src
            src = a["expert_w_down"][layer, e, f0:f0 + nf].rearrange("(q p) d -> p q d", p=P)
            return ring[i][:, 0:PIECES[j] * D].rearrange("p (q d) -> p q d", q=PIECES[j]), src

        def setup_and_norm(hTh, hTl):
            with Stage() as st:
                off = persistent_end + 2 * 4 * DC * N_TOK
                NT = 2 * DC * P // BANK
                rA, off = sb("rA", [P, P], off)
                rB, off = sb("rB", [P, P], off)
                wm, off = sb("wm", [P, NT, DC, BANK], off)
                xt, off = sb("xt", [P, TT, D], off)
                sq, off = sb("sq", [P, D], off)
                hfull, off = sb("hfull", [P, 4, BANK], off)
                ssq, off = sb("ssq", [P, 16], off)
                rstd, off = sb("rstd", [P, 16], off)
                mrow, off = sb("mrow", [P, 2, BANK], off)
                lrow, off = sb("lrow", [P, 4, HD], off)
                lsum, off = sb("lsum", [P, 8], off)
                sg, off = sb("sg", [P, 3, 2, DC], off)
                assert off <= nc.sbuf_usable_end
                s_rows, s_id, s_lam = sem(st, "s0_rows_in"), sem(st, "s0_ident_in"), sem(st, "s0_lam_in")
                s_w = [sem(st, f"s0_wmod_in{i}") for i in range(NT)]
                s_x = [sem(st, f"s0_x_in{t}") for t in range(TT)]
                cols_T, cols_ok = sem(st, "s0_cols_transposed"), sem(st, "s0_cols_copied")
                silu_ok, exp_ok = sem(st, "s0_silu_ready"), sem(st, "s0_exp_ready")
                row_mm, row_ok = sem(st, "s0_modrow_mm"), sem(st, "s0_modrow_copied")
                col_T, mod_ok = sem(st, "s0_modcol_transposed"), sem(st, "s0_mod_ready")
                ssq_ok, rstd_ok = sem(st, "s0_ssq_ready"), sem(st, "s0_rstd_ready")
                xn_ok, xT_mm, hT_ok = sem(st, "s0_xn_ready"), sem(st, "s0_x_transposed"), sem(st, "s0_hT_ready")
                d_step, p_step, lam_ok = sem(st, "s0_dve_step"), sem(st, "s0_pool_step"), sem(st, "s0_lam_exp")
                ones_ok = sem(st, "s0_ones_ready")
                hi_ok, lo_ok = sem(st, "s0_hi_ready"), [sem(st, f"s0_lo_ready{i}") for i in range(2)]
                block = st.enter_context(nc.Block())

                def low_part(eng, ops, n):
                    t0, nt = ((0, 4), (4, 4), (8, 1))[n // DC]
                    c = n % DC
                    eng.wait_ge(hi_ok, n + 1)
                    cols = slice(t0 * P, (t0 + nt) * P)
                    ops.tensor_tensor(hTl[:, c, cols], hfull[:, n % 4, 0:nt * P], hTh[:, c, cols].bitcast(F32),
                                      ALU.subtract).then_inc(lo_ok[n % 2], 1)

                @block.sync
                def _(sp):
                    sp.dma_start(ident[:], a["ident"]).then_inc(s_id, 16)
                    ra = rA[:, :]
                    sp.dma_start(ra[0:96], a["b_mod"].rearrange("l (t p) -> (l t) p", p=P)).then_inc(s_rows, 16)
                    sp.dma_start(ra[96:112], a["norm1_g"].rearrange("l (t p) -> (l t) p", p=P)).then_inc(s_rows, 16)
                    sp.dma_start(ra[112:128], a["norm2_g"].rearrange("l (t p) -> (l t) p", p=P)).then_inc(s_rows, 16)
                    rb = rB[:, :]
                    sp.dma_start(rb[0:8], a["c"].rearrange("b (t p) -> (b t) p", p=P)).then_inc(s_rows, 16)
                    sp.dma_start(rb[8:16], a["c_ctx"].rearrange("(t p) -> t p", p=P)).then_inc(s_rows, 16)
                    sp.dma_start(rb[16:24], a["pool_b"].rearrange("l g (t p) -> (l g t) p", p=P)).then_inc(s_rows, 16)
                    sp.dma_start(rb[24:32], a["pool_scale"].rearrange("l (t p) -> (l t) p", p=P)).then_inc(s_rows, 16)
                    sp.dma_start(rb[32:33], a["subln_g"]).then_inc(s_rows, 16)
                    for i in range(NT):
                        sp.dma_start(wm[:, i], a["w_mod"][0].rearrange("(c p) n -> p c n", p=P)[
                            :, :, i * BANK:(i + 1) * BANK]).then_inc(s_w[i], 16)
                    for t in range(TT):
                        sp.dma_start(xt[:, t], rows(x_in, t)).then_inc(s_x[t], 16)
                    for i, n in enumerate(("lambda_q1", "lambda_k1", "lambda_q2", "lambda_k2")):
                        sp.dma_start(lrow[:, i], a[n].partition_broadcast(P).rearrange("p a d -> p (a d)")
                                     ).then_inc(s_lam, 16)

                @block.scalar
                def _(act):
                    act.wait_ge(cols_ok, 3)
                    cc = colsB[:, 0:16].rearrange("p (s c) -> p s c", s=2)
                    nc.scalar.activation(sg[:, 0], cc, ACT.Exp, scale=-1.0).then_inc(exp_ok, 1)
                    def normalise(t):
                        act.wait_ge(rstd_ok, t + 1)
                        nc.scalar.activation(xt[:, t], xt[:, t], ACT.Copy, scale=rstd[:, t:t + 1]).then_inc(xn_ok, 1)

                    def high_part(n):
                        t0, nt = ((0, 4), (4, 4), (8, 1))[n // DC]
                        act.wait_ge(hT_ok, n + 1)
                        nc.scalar.activation(hTh[:, n % DC, t0 * P:(t0 + nt) * P], hfull[:, n % 4, 0:nt * P], ACT.Copy
                                             ).then_inc(hi_ok, 1)

                    for i in range(NT):
                        if i == NT - 1:
                            for t in range(LT // 2):
                                normalise(t)
                        act.wait_ge(row_mm, i + 1)
                        if i >= 2:
                            act.wait_ge(col_T, i - 1)
                        nc.scalar.activation(mrow[0:2, i % 2], bank[0:2, i % 2], ACT.Copy).then_inc(row_ok, 1)
                    for t in range(LT // 2, TT):
                        normalise(t)
                    for n in range(DC):
                        high_part(n)
                    act.wait_ge(ssq_ok, TT + 1)
                    nc.scalar.activation(lsum[:, 2:4], lsum[:, 0:2], ACT.Exp).then_inc(lam_ok, 1)
                    for n in range(DC, 3 * DC):
                        high_part(n)

                @block.gpsimd
                def _(pool):
                    nc.gpsimd.memset(ones[:], 1.0).then_inc(ones_ok, 1)
                    nc.gpsimd.memset(hpow[:], -0.5).then_inc(p_step, 1)
                    pool.wait_ge(p_step, 1)

                    def root(t):
                        pool.wait_ge(ssq_ok, t + 1)
                        nc.gpsimd.tensor_scalar(ssq[:, t:t + 1], ssq[:, t:t + 1], 1.0 / D, EPS, ALU.mult, ALU.add
                                                ).then_inc(p_step, 1)
                        pool.wait_ge(p_step, t + 2)
                        nc.gpsimd.tensor_tensor(rstd[:, t:t + 1], ssq[:, t:t + 1], hpow[:, 0:1], ALU.pow).then_inc(rstd_ok, 1)

                    for t in range(TT):
                        root(t)
                    for n in range(1, 3 * DC, 2):
                        low_part(pool, nc.gpsimd, n)

                @block.vector
                def _(dve):
                    step = Step(dve, d_step)
                    dve.wait_ge(cols_T, 1)
                    nc.vector.tensor_copy(colsA[:], bank[:, 2, 0:128]).then_inc(cols_ok, 1)
                    dve.wait_ge(cols_T, 2)
                    nc.vector.tensor_copy(colsB[:, 0:33], bank[:, 3, 0:33]).then_inc(cols_ok, 1)
                    dve.wait_ge(cols_ok, 2)
                    for cond in range(2):
                        nc.vector.tensor_copy(bmod2[:, :, cond], colsA[:, 0:96]).then_inc(cols_ok, 1)
                    nc.vector.tensor_scalar(sub8[:], colsB[:, 32:33], 1.0 - LAM_INIT, None, ALU.mult
                                            ).then_inc(cols_ok, 1)
                    dve.wait_ge(exp_ok, 1)
                    step.link(nc.vector.tensor_scalar(sg[:, 1], sg[:, 0], 1.0, None, ALU.add))
                    step.link(nc.vector.reciprocal(sg[:, 2], sg[:, 1]))
                    nc.vector.tensor_tensor(silu[:], colsB[:, 0:16].rearrange("p (s c) -> p s c", s=2), sg[:, 2],
                                            ALU.mult).then_inc(silu_ok, 1)
                    def squares(t):
                        dve.wait_ge(s_x[t], 16)
                        if t:
                            dve.wait_ge(ssq_ok, t)
                        nc.vector.tensor_tensor_reduce(sq[:], xt[:, t], xt[:, t], 1.0, 0.0, ALU.mult, ALU.add,
                                                       ssq[:, t:t + 1]).then_inc(ssq_ok, 1)

                    def columns(i):
                        dve.wait_ge(col_T, i + 1)
                        n = BANK // P
                        nc.vector.tensor_tensor(modc[:, n * i:n * i + n, :],
                                                bank[:, 4 + i % 2, 0:2 * n].rearrange("p (n s) -> p n s", s=2),
                                                bmod2[:, n * i:n * i + n, :], ALU.add).then_inc(mod_ok, 1)

                    for t in range(TT):
                        squares(t)
                        if t in (LT // 2 - 2, LT // 2):
                            columns((t - LT // 2) // 2 + 1)
                    columns(NT - 2)
                    columns(NT - 1)
                    dve.wait_ge(mod_ok, NT)
                    for cond in range(2):
                        nc.vector.scalar_tensor_tensor(gains[:, 0, :, cond], modc[:, SCALE1 * DC:SCALE1 * DC + DC, cond],
                                                       1.0, colsA[:, 96:96 + DC], ALU.add, ALU.mult
                                                       ).then_inc(mod_ok, 1)
                    dve.wait_ge(mod_ok, NT + 2)

                    n = 0
                    for g, (t0, nt) in enumerate(((0, 4), (4, 4), (8, 1))):
                        if g == 1:
                            dve.wait_ge(s_lam, 64)
                            dve.wait_ge(ssq_ok, TT)
                            step.link(nc.vector.tensor_tensor_reduce(sq[:, 0:HD], lrow[:, 0], lrow[:, 1], 1.0, 0.0, ALU.mult,
                                                                     ALU.add, lsum[:, 0:1]))
                            nc.vector.tensor_tensor_reduce(sq[:, 0:HD], lrow[:, 2], lrow[:, 3], 1.0, 0.0, ALU.mult, ALU.add,
                                                           lsum[:, 1:2]).then_inc(ssq_ok, 1)
                        cond = 1 if t0 == LT else 0
                        for c in range(DC):
                            dve.wait_ge(xT_mm, n + 1)
                            if n >= 4:
                                dve.wait_ge(lo_ok[n % 2], (n - 4) // 2 + 1)
                            nc.vector.tensor_scalar(hfull[:, n % 4, 0:nt * P], bank[:, n % 8, 0:nt * P],
                                                    gains[:, 0, c, cond:cond + 1],
                                                    modc[:, SHIFT1 * DC + c, cond:cond + 1], ALU.mult, ALU.add
                                                    ).then_inc(hT_ok, 1)
                            n += 1
                            if n >= 2 and n % 2 == 0:
                                low_part(dve, nc.vector, n - 2)
                    dve.wait_ge(lam_ok, 1)
                    step.link(nc.vector.tensor_tensor(lsum[:, 4:5], lsum[:, 3:4], lsum[:, 2:3], ALU.subtract))
                    step.link(nc.vector.tensor_scalar(nlam[:], lsum[:, 4:5], -LAM_INIT, None, ALU.add))

                @block.tensor
                def _(pe):
                    pe.wait_ge(s_id, 16)
                    pe.wait_ge(s_rows, 16 * 8)
                    nc.tensor.transpose(bank[:, 2, 0:128], rA[:], ident[:]).then_inc(cols_T, 1)
                    nc.tensor.transpose(bank[:, 3, 0:33], rB[0:33], ident[0:33, 0:33]).then_inc(cols_T, 1)
                    pe.wait_ge(silu_ok, 1)
                    n = BANK // P
                    for i in range(NT + 1):
                        if i < NT:
                            pe.wait_ge(s_w[i], 16)
                            if i >= 2:
                                pe.wait_ge(row_ok, i - 1)
                            for c in range(DC):
                                last = nc.tensor.matmul(bank[0:2, i % 2, :], silu[:, :, c], wm[:, i, c],
                                                        start=(c == 0), stop=(c == DC - 1))
                            last.then_inc(row_mm, 1)
                        if i:
                            pe.wait_ge(row_ok, i)
                            if i >= 3:
                                pe.wait_ge(mod_ok, i - 2)
                            for j in range(n):
                                last = nc.tensor.transpose(bank[:, 4 + (i - 1) % 2, 2 * j:2 * j + 2],
                                                           mrow[0:2, (i - 1) % 2, j * P:(j + 1) * P], ident[0:2, 0:2])
                            last.then_inc(col_T, 1)
                    n = 0
                    pe.wait_ge(cols_ok, 2)
                    pe.wait_ge(row_ok, NT)
                    pe.wait_ge(mod_ok, NT)
                    for t0, nt in ((0, 4), (4, 4), (8, 1)):
                        pe.wait_ge(xn_ok, t0 + nt)
                        for c in range(DC):
                            if n >= 8:
                                pe.wait_ge(hT_ok, n - 7)
                            for j in range(nt):
                                last = nc.tensor.transpose(bank[:, n % 8, j * P:(j + 1) * P],
                                                           xt[:, t0 + j, c * P:(c + 1) * P], ident[:])
                            last.then_inc(xT_mm, 1)
                            n += 1

        def attention(hTh, hTl, off):
            with Stage() as st:
                MA, MB = 4 * D // H, 6 * D // H
                ctab, off = sb("ctab", [P, LT, VD], off)
                stab, off = sb("stab", [P, LT, VD], off)
                wraw, off = sb("wraw", [P, 2, 2, 3 * VD], off)
                whh, off = sb("whh", [P, DC, 3 * VD], off, F32R)
                whl, off = sb("whl", [P, DC, 3 * VD], off, F32R)
                wmA, off = sb("wmA", [P, 2, MA], off)
                wmB, off = sb("wmB", [P, 2, MB], off)
                prod, off = sb("prod", [P, MB], off)
                acc, off = sb("acc", [P, 2, MA + MB], off)
                qs, off = sb("qs", [P, 2, 2, N_TOK], off, F32R)
                kk, off = sb("kk", [P, 2, KEYS + N_CTX], off, F32R)
                V, off = sb("V", [P, 10, VD], off)
                kc, off = sb("kc", [P, VD], off)
                rot, off = sb("rot", [P, 2, 2 * VD], off)
                part, off = sb("part", [P, 2, 4, 3, HD], off, F32R)
                m1, off = sb("m1", [P, 2 * VD], off)
                m2, off = sb("m2", [P, 2 * VD], off)
                P0, off = sb("P0", [P, 3, KEYS], off)
                P1, off = sb("P1", [P, KEYS], off)
                PT, off = sb("PT", [P, KEYS], off)
                ot, off = sb("ot", [P, TT, VD], off)
                nm, off = sb("nm", [P, 2], off)
                ssum, off = sb("ssum", [P, 2, 2], off)
                rec, off = sb("rec", [P, TT, 2], off)
                cneg, off = sb("cneg", [P, 1], off)
                assert off <= nc.sbuf_usable_end, off
                S = {}
                for n in ("tab_in kc_in vc_in kv_out o_out qkv_mm v_done rot_done rot_T qk_evac S_mm hi_ok lo_ok "
                          "mx_done exp_done comb_step a_done aT_mm PT_ok pv_mm o_evac wmA_used wmB_used prod_ok "
                          "modcol_mm modc_done rope_part w_hi w_lo").split():
                    S[n] = sem(st, "at_" + n)
                w_in = [sem(st, f"at_w_in{i}") for i in range(2)]
                wmA_in = [sem(st, f"at_wmA_in{i}") for i in range(2)]
                wmB_in = [sem(st, f"at_wmB_in{i}") for i in range(2)]
                block = st.enter_context(nc.Block())
                LAST = TT - 1
                V_CUT = 4
                CUTS = (12, 18)
                NT_A = 3 * LT + 1
                NR = TT + 2
                w = a["attn_wqkv"][0].rearrange("(c p) (i n) -> p c i n", p=P, i=3)
                wmodA = a["w_mod"][0].rearrange("(c p) n -> p c n", p=P)[:, :, 2 * D:]
                wmodB = a["w_mod"][1].rearrange("(c p) n -> p c n", p=P)
                kcd = a["cache_k"][0, 0].rearrange("t h d -> t (h d)")
                vcd = a["cache_v"][0, 0].rearrange("t h d -> t (h d)")
                nkd = out["new_cache_k"][0, 0].rearrange("t h d -> t (h d)")
                nvd = out["new_cache_v"][0, 0].rearrange("t h d -> t (h d)")

                @block.sync
                def _(sp):
                    def load_w(h, i):
                        for j in range(2):
                            sp.dma_start(wraw[:, i % 2, j].rearrange("p (i n) -> p i n", i=3),
                                         w[:, 2 * i + j, :, bass.ds(h * VD, VD)]).then_inc(w_in[i % 2], 16)

                    def load_kc(h):
                        sp.dma_start(kc[:], kcd[:, bass.ds(h * VD, VD)]).then_inc(S["kc_in"], 16)

                    def load_vc(h):
                        sp.dma_start(V[:, LT], vcd[:, bass.ds(h * VD, VD)]).then_inc(S["vc_in"], 16)

                    def load_wmA(h, i):
                        sp.dma_start(wmA[:, i], wmodA[:, i, bass.ds(h * MA, MA)]).then_inc(wmA_in[i], 16)

                    def load_wmB(h):
                        for i in range(DC):
                            sp.wait_ge(S["wmB_used"], DC * h + i + 1)
                            sp.dma_start(wmB[:, i % 2], wmodB[:, i, bass.ds(h * MB, MB)]).then_inc(wmB_in[i % 2], 16)

                    def store_kv(h):
                        sp.wait_ge(S["rot_done"], TT * h + TT)
                        sp.dma_start(nkd[:, bass.ds(h * VD, VD)], rot[:, LAST % 2, VD:2 * VD]).then_inc(S["kv_out"], 16)
                        sp.wait_ge(S["v_done"], TT * h + TT)
                        sp.dma_start(nvd[:, bass.ds(h * VD, VD)], V[:, LT + 1]).then_inc(S["kv_out"], 16)

                    def store_o(h):
                        sp.wait_ge(S["o_evac"], TT * h + TT + 1)
                        for t in range(2):
                            src, dst = (ot[:, 0:LT], oscr[0]) if t == 0 else (ot[:, LT:TT], oscr[1])
                            sp.dma_start(dst.rearrange("(t p) d -> p t d", p=P)[:, :, bass.ds(h * VD, VD)], src
                                         ).then_inc(S["o_out"], 16)

                    sp.sem_inc(S["kv_out"], 1)
                    sp.sem_inc(S["o_out"], 1)
                    load_w(0, 0)
                    load_w(0, 1)
                    for i in (2, 3):
                        sp.wait_ge(S["w_lo"], i - 1)
                        load_w(0, i)
                    load_kc(0)
                    load_wmA(0, 0)
                    load_wmA(0, 1)
                    load_vc(0)
                    with sp.Fori(0, H - 1) as h:
                        sp.wait_ge(S["w_lo"], 4 * h + 4)
                        load_w(h + 1, 0)
                        load_w(h + 1, 1)
                        load_wmB(h)
                        store_kv(h)
                        sp.wait_ge(S["rot_T"], NR * h + 1)
                        load_kc(h + 1)
                        for i in (2, 3):
                            sp.wait_ge(S["w_lo"], 4 * h + 3 + i)
                            load_w(h + 1, i)
                        sp.wait_ge(S["wmA_used"], DC * h + DC)
                        load_wmA(h + 1, 0)
                        load_wmA(h + 1, 1)
                        sp.wait_ge(S["pv_mm"], TT * h + TT)
                        load_vc(h + 1)
                        store_o(h)
                    load_wmB(H - 1)
                    store_kv(H - 1)
                    store_o(H - 1)
                    sp.wait_ge(S["kv_out"], 32 * H + 1)
                    sp.wait_ge(S["o_out"], 32 * H + 1)

                @block.gpsimd
                def _(pool):
                    def split(i, raw_in, step):
                        pool.wait_ge(w_in[i % 2], raw_in)
                        nc.gpsimd.tensor_tensor(whh[:, 2 * i:2 * i + 2], wraw[:, i % 2],
                                                ones[:, 0:1].unsqueeze(1).to_broadcast([P, 2, 3 * VD]), ALU.mult
                                                ).then_inc(S["w_hi"], 1)
                        pool.wait_ge(S["w_hi"], step)
                        nc.gpsimd.tensor_tensor(whl[:, 2 * i:2 * i + 2], wraw[:, i % 2], whh[:, 2 * i:2 * i + 2].bitcast(F32),
                                                ALU.subtract).then_inc(S["w_lo"], 1)

                    def modulate(h):
                        for i in range(DC):
                            pool.wait_ge(wmB_in[i % 2], 8 * DC * h + 16 * (i // 2) + 16)
                            pool.wait_ge(S["wmB_used"], DC * h + i + 2)
                            if i == 0:
                                pool.wait_ge(S["modcol_mm"], h + 1)
                            accs = acc[:, 0, MA:MA + MB], acc[:, 1, MA:MA + MB]
                            dsts = accs if i == 0 else (prod[:], wmB[:, i % 2])
                            nc.gpsimd.tensor_tensor(dsts[0], wmB[:, i % 2], silu[:, 0, i:i + 1].to_broadcast([P, MB]), ALU.mult
                                                    ).then_inc(S["prod_ok"], 1)
                            pool.wait_ge(S["prod_ok"], 2 * DC * h + 2 * i + 1)
                            last = nc.gpsimd.tensor_tensor(dsts[1], wmB[:, i % 2], silu[:, 1, i:i + 1].to_broadcast([P, MB]), ALU.mult)
                            last.then_inc(S["prod_ok"], 1)
                            pool.wait_ge(S["prod_ok"], 2 * DC * h + 2 * i + 2)
                            if i:
                                for x, y in zip(accs, dsts):
                                    last = nc.gpsimd.tensor_tensor(x, x, y, ALU.add)
                                last.then_inc(S["wmB_used"], 1)
                            else:
                                pool.sem_inc(S["wmB_used"], 1)

                    pool.sem_inc(S["modcol_mm"], 1)
                    pool.sem_inc(S["wmB_used"], 2)
                    with pool.Fori(0, H - 1) as h:
                        modulate(h)
                        pool.wait_ge(S["qkv_mm"], TT * h + TT)
                        for i in range(4):
                            split(i, 64 * h + 96 + 32 * (i // 2), 4 * h + 5 + i)
                    modulate(H - 1)

                @block.tensor
                def _(pe):
                    def qkv(h, t, first=0, stop=3 * DC):
                        if t >= 2:
                            pe.wait_ge(S["v_done"], TT * h + t - 1)
                        elif t == 1:
                            pe.wait_ge(S["o_evac"], TT * h + 1)
                        for n in range(first, stop):
                            c = n // 3
                            if t == 0 and n % 6 == 0:
                                pe.wait_ge(S["w_lo"], 4 * h + n // 6 + 1)
                            x, y = ((hTh, whh), (hTh, whl), (hTl, whh))[n % 3]
                            last = nc.tensor.matmul(bank[:, 6 + t % 2, 0:3 * VD], x[:, c, t * P:(t + 1) * P], y[:, c],
                                                    start=(n == 0), stop=(n == 3 * DC - 1))
                        if stop == 3 * DC:
                            last.then_inc(S["qkv_mm"], 1)

                    def turn_q(src, b):
                        for s in range(2):
                            for m in range(2):
                                last = nc.tensor.transpose(bank[:, b, (2 * s + m) * P:(2 * s + m + 1) * P],
                                                           src[:, s, m * HD:(m + 2) * HD], ident[:])
                        return last

                    def turn_k(src, b):
                        for s in range(2):
                            last = nc.tensor.transpose(bank[:, b, s * P:(s + 1) * P], src[:, 2 + s, 0:2 * HD], ident[:])
                        return last

                    def parts(i):
                        return part[:, i % 2].rearrange("p i m d -> p i (m d)").bitcast(F32)

                    def turn(h, i):
                        pe.wait_ge(S["lo_ok"], (TT + 1) * h + i + 1)
                        if i >= 2:
                            pe.wait_ge(S["qk_evac"], NR * h + i - 1)
                        elif i == 1:
                            pe.wait_ge(S["modc_done"], h + 1)
                        if i:
                            turn_q(parts(i), i % 2)
                        turn_k(parts(i), 3 + i % 2).then_inc(S["rot_T"], 1)

                    def turn_ctx(h, i):
                        if i == 0:
                            pe.wait_ge(S["lo_ok"], (TT + 1) * h + TT + 1)
                            turn_q(parts(TT), 7).then_inc(S["rot_T"], 1)
                        else:
                            pe.wait_ge(S["qk_evac"], NR * h + TT + 1)
                            turn_k(parts(TT), 7).then_inc(S["rot_T"], 1)

                    def scores(h, n, s):
                        if n:
                            pe.wait_ge(S["exp_done"], 2 * TT * h + 2 * n + s - 1)
                        elif s == 0:
                            pe.wait_ge(S["qk_evac"], NR * h + TT)
                        blocks = [(b, 384 * b, 384) for b in range(3)] if n < LAST else [(0, KEYS, N_CTX)]
                        for b, k0, width in blocks:
                            for m in range(2):
                                last = nc.tensor.matmul(bank[:, 3 * s + b, 0:width], qs[:, s, m, n * P:(n + 1) * P],
                                                        kk[:, s, k0:k0 + width], start=(m == 0), stop=(m == 1))
                        last.then_inc(S["S_mm"], 1)

                    def turn_a(h, n, i):
                        if i == 0:
                            pe.wait_ge(S["a_done"], TT * h + n + 2)
                        if n == 0 and i == 0:
                            pe.wait_ge(S["v_done"], TT * h + TT)
                        else:
                            pe.wait_ge(S["PT_ok"], NT_A * h + 3 * n + i)
                        tiles = ((0, 4), (4, 8), (8, 9))[i] if n < LAST else (0, 1)
                        for j in range(*tiles):
                            last = nc.tensor.transpose(bank[:, 6, (j - tiles[0]) * P:(j - tiles[0] + 1) * P],
                                                       P0[:, n % 3, j * P:(j + 1) * P], ident[:])
                        last.then_inc(S["aT_mm"], 1)

                    def times_v(h, n, first, stop):
                        if n == 0 and first == 0:
                            pe.wait_ge(S["vc_in"], 16 * h + 16)
                            pe.wait_ge(S["qk_evac"], NR * h + NR)
                        if first == 0:
                            pe.wait_ge(S["o_evac"], TT * h + n + 1)
                        tiles = range(LT + 1) if n < LAST else [LT + 1]
                        for i, j in list(enumerate(tiles))[first:stop]:
                            if i in (0, 4, 8):
                                pe.wait_ge(S["PT_ok"], NT_A * h + 3 * n + i // 4 + 1)
                            last = nc.tensor.matmul(bank[:, 7, 0:VD], PT[:, i * P:(i + 1) * P], V[:, j],
                                                    start=(i == 0), stop=(i == len(tiles) - 1))
                        if stop > LT:
                            last.then_inc(S["pv_mm"], 1)

                    SUMS = 2 * (MA + MB) // P

                    def sums(h, first, stop):
                        if first == 0:
                            pe.wait_ge(S["wmA_used"], DC * h + DC)
                            pe.wait_ge(S["wmB_used"], DC * h + DC + 2)
                        for i in range(first, stop):
                            j, cond = i // 2, i % 2
                            last = nc.tensor.matmul(bank[:, 1, i:i + 1], acc[:, cond, j * P:(j + 1) * P], ones[:, 0:1],
                                                    start=True, stop=True)
                        if stop == SUMS:
                            last.then_inc(S["modcol_mm"], 1)

                    with pe.Fori(0, H) as h:
                        for t in range(LT):
                            qkv(h, t)
                            turn(h, t)
                        qkv(h, LAST, 0, CUTS[0])
                        turn(h, LT)
                        qkv(h, LAST, *CUTS)
                        for n in range(TT + 2):
                            if n < TT:
                                scores(h, n, 0)
                            if n == 2:
                                turn_ctx(h, 1)
                            if n >= 2:
                                turn_a(h, n - 2, 0)
                            if n < TT:
                                scores(h, n, 1)
                            if n == 0:
                                qkv(h, LAST, CUTS[1])
                            if n == 1:
                                turn_ctx(h, 0)
                            if n == TT:
                                sums(h, 0, 8)
                            if n == TT + 1:
                                sums(h, 8, SUMS)
                            if 2 <= n <= TT:
                                turn_a(h, n - 2, 1)
                                times_v(h, n - 2, 0, V_CUT)
                                turn_a(h, n - 2, 2)
                            if n >= 2:
                                times_v(h, n - 2, V_CUT if n <= TT else 0, LT + 1)

                @block.scalar
                def _(act):
                    def values(h, t):
                        if t < LAST:
                            act.wait_ge(S["rope_part"], LT * h + t + 1)
                        else:
                            act.wait_ge(S["rot_done"], TT * h + TT)
                            act.wait_ge(S["kv_out"], 32 * h + 1)
                        nc.scalar.activation(V[:, t if t < LT else LT + 1], bank[:, 6 + t % 2, 2 * VD:3 * VD], ACT.Copy
                                             ).then_inc(S["v_done"], 1)

                    def high(h, i):
                        if i == 0:
                            act.wait_ge(S["kc_in"], 16 * h + 16)
                            nc.scalar.activation(part[:, 0, 2:4, 0], kc[:].rearrange("p (i d) -> p i d", d=HD), ACT.Copy
                                                 ).then_inc(S["hi_ok"], 1)
                            return
                        act.wait_ge(S["rot_done"], TT * h + i)
                        if i >= 2:
                            act.wait_ge(S["rot_T"], NR * h + i - 1)
                        r = rot[:, (i - 1) % 2].rearrange("p (i d) -> p i d", d=HD).unsqueeze(2).to_broadcast([P, 4, 2, HD])
                        nc.scalar.activation(part[:, i % 2, :, 0:3:2], r, ACT.Copy).then_inc(S["hi_ok"], 1)

                    def q_out(t, b):
                        return nc.scalar.activation(qs[:, :, :, t * P:(t + 1) * P],
                                                    bank[:, b, :].rearrange("p (s m n) -> p s m n", s=2, m=2), ACT.Copy,
                                                    scale=HD ** -0.5)

                    def k_out(k0, b):
                        return nc.scalar.activation(kk[:, :, k0:k0 + P], bank[:, b, 0:2 * P].rearrange("p (s n) -> p s n", s=2),
                                                    ACT.Copy)

                    def evac(h, i):
                        act.wait_ge(S["rot_T"], NR * h + i + 1)
                        if i:
                            q_out(i - 1, i % 2)
                        k_out((i - 1) * P if i else N_LAT, 3 + i % 2).then_inc(S["qk_evac"], 1)

                    def evac_ctx(h, i):
                        act.wait_ge(S["rot_T"], NR * h + TT + i + 1)
                        (k_out(KEYS, 7) if i else q_out(LAST, 7)).then_inc(S["qk_evac"], 1)

                    def exp(h, n, s):
                        act.wait_ge(S["mx_done"], 2 * TT * h + 2 * n + s + 1)
                        dst = P0[:, n % 3] if s == 0 else P1
                        if s == 0 and n >= 3:
                            act.wait_ge(S["aT_mm"], NT_A * h + 3 * n - 6)
                        if s == 1:
                            act.wait_ge(S["a_done"], TT * h + n + 1)
                        if n < LAST:
                            nc.scalar.activation(dst[:, 0:KEYS].rearrange("p (b n) -> p b n", b=3),
                                                 bank[:, 3 * s:3 * s + 3, 0:384], ACT.Exp, bias=nm[:, s:s + 1],
                                                 accum_out=ssum[:, n % 2, s:s + 1]).then_inc(S["exp_done"], 1)
                        else:
                            nc.scalar.activation(dst[:, 0:N_CTX], bank[:, 3 * s, 0:N_CTX], ACT.Exp, bias=nm[:, s:s + 1],
                                                 accum_out=ssum[:, n % 2, s:s + 1]).then_inc(S["exp_done"], 1)

                    def aT_out(h, n, i):
                        act.wait_ge(S["aT_mm"], NT_A * h + 3 * n + i + 1)
                        lo, hi = ((0, 512), (512, 1024), (1024, KEYS))[i] if n < LAST else (0, N_CTX)
                        nc.scalar.activation(PT[:, lo:hi], bank[:, 6, 0:hi - lo], ACT.Copy).then_inc(S["PT_ok"], 1)

                    act.dma_start(ctab[:], a["rope_cos"].rearrange("(t p) n -> p t n", p=P)).then_inc(S["tab_in"], 16)
                    act.dma_start(stab[:], a["rope_sin"].rearrange("(t p) n -> p t n", p=P)).then_inc(S["tab_in"], 16)
                    for i in range(4):
                        act.wait_ge(w_in[i % 2], 32 * (i // 2) + 32)
                        nc.scalar.activation(whh[:, 2 * i:2 * i + 2], wraw[:, i % 2], ACT.Copy).then_inc(S["w_hi"], 1)
                    act.sem_inc(S["o_evac"], 1)
                    with act.Fori(0, H) as h:
                        high(h, 0)
                        for t in range(LT):
                            values(h, t)
                            high(h, t + 1)
                            if 1 <= t < DC - 1:
                                act.wait_ge(S["wmA_used"], DC * h + t)
                                act.dma_start(wmA[:, (t + 1) % 2], wmodA[:, t + 1, bass.ds(h * MA, MA)]
                                              ).then_inc(wmA_in[(t + 1) % 2], 16)
                            evac(h, t)
                        evac(h, LT)
                        for n in range(TT + 2):
                            if 1 <= n <= TT:
                                exp(h, n - 1, 1)
                            if n == 1:
                                values(h, LAST)
                                high(h, TT)
                            if n == 2:
                                evac_ctx(h, 1)
                            if n >= 2:
                                aT_out(h, n - 2, 0)
                            if n < TT:
                                exp(h, n, 0)
                            if n == 1:
                                evac_ctx(h, 0)
                            if 2 <= n <= TT:
                                aT_out(h, n - 2, 1)
                                aT_out(h, n - 2, 2)
                            if n >= 2:
                                m = n - 2
                                act.wait_ge(S["pv_mm"], TT * h + m + 1)
                                if m == 0:
                                    act.wait_ge(S["o_out"], 32 * h + 1)
                                nc.scalar.activation(ot[:, m], bank[:, 7, 0:VD], ACT.Copy, scale=rec[:, m, 0:1]
                                                     ).then_inc(S["o_evac"], 1)

                @block.vector
                def _(dve):
                    def rotate(h, t):
                        dve.wait_ge(S["qkv_mm"], TT * h + t + 1)
                        src = bank[:, 6 + t % 2, 0:2 * VD]
                        if t == 0:
                            dve.wait_ge(S["kv_out"], 32 * h + 1)
                        if t == LAST:
                            nc.vector.tensor_copy(rot[:, t % 2], src).then_inc(S["rot_done"], 1)
                            return
                        if t:
                            dve.wait_ge(S["rot_done"], TT * h + t)
                        nc.vector.tensor_tensor(m1[:].rearrange("p (i n) -> p i n", i=2), src.rearrange("p (i n) -> p i n", i=2),
                                                ctab[:, t].unsqueeze(1).to_broadcast([P, 2, VD]), ALU.mult)
                        for i in range(2):
                            sw = src.rearrange("p (i b two r) -> p i b two r", i=2, two=2, r=16)[:, :, :, 1 - i]
                            dw = m2[:].rearrange("p (i b two r) -> p i b two r", i=2, two=2, r=16)[:, :, :, i]
                            tw = stab[:, t].rearrange("p (b two r) -> p b two r", two=2, r=16)[:, :, i]
                            last = nc.vector.tensor_tensor(dw, sw, tw.unsqueeze(1).to_broadcast([P, 2, 4, 16]), ALU.mult)
                        last.then_inc(S["rope_part"], 1)
                        dve.wait_ge(S["rope_part"], LT * h + t + 1)
                        nc.vector.tensor_tensor(rot[:, t % 2], m1[:], m2[:], ALU.add).then_inc(S["rot_done"], 1)

                    def low(h, i):
                        dve.wait_ge(S["hi_ok"], (TT + 1) * h + i + 1)
                        lo = 0 if i else 2
                        src = rot[:, (i - 1) % 2] if i else kc[:]
                        nc.vector.tensor_tensor(part[:, i % 2, lo:4, 1], src.rearrange("p (i d) -> p i d", d=HD),
                                                part[:, i % 2, lo:4, 0].bitcast(F32), ALU.subtract).then_inc(S["lo_ok"], 1)

                    def modulate(h, c):
                        dve.wait_ge(wmA_in[c % 2], 8 * DC * h + 16 * (c // 2) + 16)
                        if c:
                            dve.wait_ge(S["wmA_used"], DC * h + c)
                        for cond in range(2):
                            dst, k = acc[:, cond, 0:MA], silu[:, cond, c:c + 1]
                            last = (nc.vector.scalar_tensor_tensor(dst, wmA[:, c % 2], k, dst, ALU.mult, ALU.add) if c
                                    else nc.vector.tensor_scalar(dst, wmA[:, c % 2], k, None, ALU.mult))
                        last.then_inc(S["wmA_used"], 1)

                    def row_max(h, n, s):
                        dve.wait_ge(S["S_mm"], 2 * TT * h + 2 * n + s + 1)
                        src = bank[:, 3 * s:3 * s + 3, 0:384] if n < LAST else bank[:, 3 * s, 0:N_CTX]
                        nc.vector.tensor_reduce(nm[:, s:s + 1], src, AX.XY if n < LAST else AX.X, ALU.max, negate=True
                                                ).then_inc(S["mx_done"], 1)

                    def difference(h, n):
                        dve.wait_ge(S["exp_done"], 2 * TT * h + 2 * n + 2)
                        step = Step(dve, S["comb_step"], 2 * TT * h + 2 * n)
                        step.link(nc.vector.reciprocal(rec[:, n], ssum[:, n % 2]))
                        step.link(nc.vector.scalar_tensor_tensor(cneg[:], rec[:, n, 1:2], ssum[:, n % 2, 0:1], nlam[:],
                                                                 ALU.mult, ALU.mult))
                        kw = KEYS if n < LAST else N_CTX
                        nc.vector.scalar_tensor_tensor(P0[:, n % 3, 0:kw], P1[:, 0:kw], cneg[:], P0[:, n % 3, 0:kw],
                                                       ALU.mult, ALU.add).then_inc(S["a_done"], 1)

                    dve.sem_inc(S["modc_done"], 1)
                    dve.sem_inc(S["a_done"], 1)
                    for i in range(4):
                        dve.wait_ge(S["w_hi"], i + 1)
                        nc.vector.tensor_tensor(whl[:, 2 * i:2 * i + 2], wraw[:, i % 2], whh[:, 2 * i:2 * i + 2].bitcast(F32),
                                                ALU.subtract).then_inc(S["w_lo"], 1)
                    dve.wait_ge(S["tab_in"], 32)
                    with dve.Fori(0, H) as h:
                        for t in range(LT):
                            low(h, t)
                            rotate(h, t)
                            modulate(h, t)
                        low(h, LT)
                        for n in range(TT + 1):
                            if n < TT:
                                row_max(h, n, 0)
                            if n == 1:
                                low(h, TT)
                            if n:
                                difference(h, n - 1)
                            if n < TT:
                                row_max(h, n, 1)
                            if n == 0:
                                rotate(h, LAST)
                        dve.wait_ge(S["modcol_mm"], h + 2)
                        for first, n, lo in ((2 * DC + MA // P * h, MA // P, 0), (SECT + MB // P * h, MB // P, MA // P)):
                            last = nc.vector.tensor_tensor(modc[:, bass.ds(first, n), :],
                                                           bank[:, 1, 2 * lo:2 * (lo + n)].rearrange("p (n s) -> p n s", s=2),
                                                           bmod2[:, bass.ds(first, n), :], ALU.add)
                        last.then_inc(S["modc_done"], 1)

        def mixer_and_route(layer, pT, off):
            attn = layer == 0
            cond_of = [0] * LT + [1]
            HALF, HI = N_LAT // 2, 32
            PB = (0, 0) if attn else (0, 2)
            ahead = 1 if attn else 2
            with Stage() as st:
                xt, off = sb(f"mx_xt{layer}", [P, 2, D], off)
                xn, off = sb(f"mx_xn{layer}", [P, 2, D], off)
                h2, off = sb(f"mx_h2{layer}", [P, 2, DC, P], off)
                gA, off = sb(f"mx_gA{layer}", [P, 2, D], off)
                wr, off = sb(f"mx_wr{layer}", [P, DC, E], off)
                anti, off = sb(f"mx_anti{layer}", [P, P], off)
                sm, off = sb(f"mx_sm{layer}", [P, 2, 4, E], off)
                st1, off = sb(f"mx_st{layer}", [P, TT, 8], off)
                if attn:
                    woh, at = sb("mx_woh", [P, H, D], big_at, F32R)
                    woraw = [sb("mx_woraw0", [P, D], at)[0][:]]
                    assert at + 4 * D <= ring_at
                    wol, off = sb("mx_wol", [P, H, D], off, F32R)
                    t, off = sb("mx_woraw1", [P, D], off)
                    woraw += [xn[:, 0], xn[:, 1], h2[:, 0].rearrange("p c n -> p (c n)"), h2[:, 1].rearrange("p c n -> p (c n)"), t[:]]
                    NRAW = len(woraw)

                    def raw_of(i):
                        return i if i < NRAW else (0, NRAW - 1)[i - NRAW]
                    oin, off = sb("mx_oin", [P, 2, D], off)
                    om, off = sb("mx_om", [P, D], off)
                    oTh, off = sb("mx_oTh", [P, 2, H, P], off, F32R)
                    oTl, off = sb("mx_oTl", [P, 2, H, P], off, F32R)
                    osm, off = sb("mx_osm", [P, 2, 2, H], off)
                else:
                    pw, off = sb("mx_pw", [P, 4, 2, GROUP], off)
                    gB, off = sb("mx_gB", [P, 2, D], off)
                    pcol, off = sb("mx_pcol", [P, 2, DC, 2], off)
                dg, off = sb(f"mx_dg{layer}", [P, 2, 4, P], off)
                ap, off = sb(f"mx_ap{layer}", [P, 2, HI + E], off)
                af, off = sb(f"mx_af{layer}", [P, HALF + N_CTX], off)
                rb, off = sb(f"mx_rb{layer}", [P, 2 * E], off)
                mk, off = sb(f"mx_mk{layer}", [P, 3, E], off)
                vv, off = sb(f"mx_vv{layer}", [P, P], off)
                ii, off = sb(f"mx_ii{layer}", [P, P], off, U32)
                fi, off = sb(f"mx_fi{layer}", [P, P], off)
                vc, off = sb(f"mx_vc{layer}", [P, CAP_C], off)
                ic, off = sb(f"mx_ic{layer}", [P, CAP_C], off, U32)
                fc, off = sb(f"mx_fc{layer}", [P, CAP_C], off)
                assert off <= nc.sbuf_usable_end, off
                S = {}
                for n in ("w_in wr_in dg_ok bc_mm bc_ok om_ok oT_mm oT_ok mm_done tmp_ok x_ok ssq_ok "
                          "rstd_ok xn_ok xT_mm h2_ok lg_mm lmax_ok lexp_ok aff_ok affT_mm af_ok dve_step pool_step "
                          "top_mm wo_hi wo_lo oTl_ok anti_in top_lists xb_ok oss_ok orstd_ok xu").split():
                    S[n] = sem(st, f"mx{layer}_" + n)
                x_in_s = [sem(st, f"mx{layer}_x_in{i}") for i in range(2)]
                wo_in = [sem(st, f"mx{layer}_wo_in{i}") for i in range(H if attn else 0)]
                o_in = [sem(st, f"mx{layer}_o_in{i}") for i in range(2)]
                x_out = [sem(st, f"mx{layer}_x_out{i}") for i in range(2)]
                xn_out = [sem(st, f"mx{layer}_xn_out{i}") for i in range(2)]
                block = st.enter_context(nc.Block())
                g2 = 2 * layer + 1
                base = layer * SECT
                NB = 2 if attn else 4
                x_src = x_in if attn else xres

                @block.sync
                def _(sp):
                    sp.dma_start(wr[:], a["router_w"][layer].rearrange("(c p) e -> p c e", p=P)).then_inc(S["wr_in"], 16)
                    sp.dma_start(anti[:], a["anti"]).then_inc(S["anti_in"], 16)
                    for t in range(2):
                        if attn:
                            sp.dma_start(oin[:, t], rows(oscr, t)).then_inc(o_in[t], 16)
                        sp.dma_start(xt[:, t], rows(x_src, t)).then_inc(x_in_s[t], 16)
                    if attn:
                        for i in range(H):
                            j = raw_of(i)
                            if i >= NRAW:
                                sp.wait_ge(S["wo_lo"], j + 1)
                            sp.dma_start(woraw[j], a["attn_wo"][0, i * P:(i + 1) * P]).then_inc(wo_in[i], 16)
                    else:
                        sp.dma_start(pw[:], a["pool_w"][0].rearrange("g (c p) d -> p g c d", p=P)).then_inc(S["w_in"], 16)
                    for t in range(TT):
                        if attn and t + 2 < TT:
                            sp.wait_ge(S["om_ok"], t + 1)
                            sp.dma_start(oin[:, t % 2], rows(oscr, t + 2)).then_inc(o_in[t % 2], 16)
                        sp.wait_ge(S["x_ok"], t + 1)
                        sp.dma_start(rows(xres, t), xt[:, t % 2]).then_inc(x_out[t % 2], 16)
                        sp.wait_ge(S["xn_ok"], t + 1)
                        sp.dma_start(rows(xnrm, t), xn[:, t % 2]).then_inc(xn_out[t % 2], 16)
                        if t + 2 < TT:
                            sp.wait_ge(x_out[t % 2], 16 * (t // 2 + 1))
                            sp.dma_start(xt[:, t % 2], rows(x_src, t + 2)).then_inc(x_in_s[t % 2], 16)
                    for i in range(RING_EARLY[layer]):
                        dst, src = ring_source(layer, 0, i)
                        sp.dma_start(dst, src).then_inc(ring_in[i], 16)
                    sp.wait_ge(x_out[0], 16 * 5)
                    sp.wait_ge(x_out[1], 16 * 4)
                    sp.wait_ge(xn_out[0], 16 * 5)
                    sp.wait_ge(xn_out[1], 16 * 4)

                @block.tensor
                def _(pe):
                    n = 0
                    for b in range(NB):
                        if b >= 1:
                            pe.wait_ge(S["bc_ok"], b)
                        for i in range(DC // 4):
                            pe.wait_ge(S["dg_ok"], n + 1)
                            nc.tensor.matmul(bank[:, i, :], ones[:], dg[:, n % 2].rearrange("p c n -> p (c n)"),
                                             start=True, stop=True).then_inc(S["bc_mm"], 1)
                            n += 1
                    pe.wait_ge(S["bc_ok"], NB)
                    if not attn:
                        pe.wait_ge(S["w_in"], 16)
                    pe.wait_ge(S["wr_in"], 16)

                    def turn_o(t):
                        pe.wait_ge(S["om_ok"], t + 1)
                        if t:
                            pe.wait_ge(S["oTl_ok"], t)
                        for c in range(H):
                            last = nc.tensor.transpose(bank[:, 2 + c // 4, (c % 4) * P:(c % 4 + 1) * P],
                                                       om[:, c * P:(c + 1) * P], ident[:])
                        last.then_inc(S["oT_mm"], 1)

                    def product(t):
                        b0 = PB[t % 2]
                        if t >= ahead:
                            pe.wait_ge(S["tmp_ok"], t - ahead + 1)
                        if attn:
                            pe.wait_ge(S["oTl_ok"], t + 1)
                            for c in range(H):
                                if t == 0:
                                    pe.wait_ge(S["wo_lo"], c + 1)
                                for k, (x, y) in enumerate(((oTh, woh), (oTh, wol), (oTl, woh))):
                                    for b in range(2):
                                        last = nc.tensor.matmul(bank[:, b0 + b, :], x[:, t % 2, c], y[:, c, b * 512:(b + 1) * 512],
                                                                start=(c == 0 and k == 0), stop=(c == H - 1 and k == 2))
                        else:
                            for g in range(4):
                                for c in range(2):
                                    last = nc.tensor.matmul(bank[:, b0 + g // 2, (g % 2) * GROUP:(g % 2 + 1) * GROUP],
                                                            pT[:, 2 * g + c, t], pw[:, g, c], start=(c == 0), stop=(c == 1))
                        last.then_inc(S["mm_done"], 1)

                    def turn_x(t):
                        pe.wait_ge(S["xn_ok"], t + 1)
                        if t:
                            pe.wait_ge(S["h2_ok"], t)
                        for c in range(DC):
                            last = nc.tensor.transpose(bank[:, 4 + c // 4, (c % 4) * P:(c % 4 + 1) * P],
                                                       xn[:, t % 2, c * P:(c + 1) * P], ident[:])
                        last.then_inc(S["xT_mm"], 1)

                    def router(t):
                        pe.wait_ge(S["h2_ok"], t + 1)
                        if t:
                            pe.wait_ge(S["lexp_ok"], t)
                        for c in range(DC):
                            last = nc.tensor.matmul(bank[:, 6, 0:E], h2[:, t % 2, c], wr[:, c], start=(c == 0), stop=(c == DC - 1))
                        last.then_inc(S["lg_mm"], 1)

                    def turn_aff(t):
                        pe.wait_ge(S["aff_ok"], t + 1)
                        if t:
                            pe.wait_ge(S["af_ok"], t)
                        m = HI + E if LT // 2 <= t < LT else E
                        nc.tensor.transpose(bank[0:m, 7, 0:P], ap[:, t % 2, 0:m], ident[:]).then_inc(S["affT_mm"], 1)

                    if attn:
                        turn_o(0)
                    for s in range(TT + 3):
                        if s < TT:
                            product(s)
                        if attn and s + 1 < TT:
                            turn_o(s + 1)
                        if 1 <= s <= TT:
                            turn_x(s - 1)
                        if 2 <= s <= TT + 1:
                            router(s - 2)
                        if s >= 3:
                            turn_aff(s - 3)
                    pe.wait_ge(S["top_lists"], 1)
                    nc.tensor.transpose(bank[:, 0, 0:HI + E], vv[0:HI + E], ident[0:HI + E, 0:HI + E])
                    nc.tensor.transpose(bank[:, 0, 64:64 + HI + E], fi[0:HI + E], ident[0:HI + E, 0:HI + E])
                    nc.tensor.transpose(bank[0:CAP_C, 0, 128:128 + E], vc[0:E], ident[0:E, 0:E])
                    nc.tensor.transpose(bank[0:CAP_C, 0, 160:160 + E], fc[0:E], ident[0:E, 0:E]).then_inc(S["top_mm"], 1)
                    pe.wait_ge(S["anti_in"], 16)
                    pe.wait_ge(S["top_lists"], 2)
                    nc.tensor.matmul(bank[:, 1, 0:2 * E], anti[:], rb[:], start=True, stop=True).then_inc(S["top_mm"], 1)

                @block.gpsimd
                def _(pool):
                    k = 0
                    def root(dst, src, n, width, done):
                        nonlocal k
                        nc.gpsimd.tensor_scalar(src, src, 1.0 / width, EPS, ALU.mult, ALU.add).then_inc(S["pool_step"], 1)
                        k += 1
                        pool.wait_ge(S["pool_step"], k)
                        nc.gpsimd.tensor_tensor(dst, src, hpow[:, 0:n], ALU.pow).then_inc(done, 1)

                    def head_norm(t):
                        pool.wait_ge(S["oss_ok"], t + 1)
                        root(osm[:, t % 2, 1], osm[:, t % 2, 0], H, VD, S["orstd_ok"])

                    if attn:
                        head_norm(0)
                    for t in range(TT):
                        if attn and t + 1 < TT:
                            head_norm(t + 1)
                        if not attn:
                            pool.wait_ge(S["bc_ok"], NB)
                            pool.wait_ge(x_in_s[t % 2], 16 * (t // 2 + 1))
                            nc.gpsimd.tensor_tensor(xt[:, t % 2], xt[:, t % 2], gB[:, cond_of[t]], ALU.add).then_inc(S["xb_ok"], 1)
                        pool.wait_ge(S["ssq_ok"], t + 1)
                        root(st1[:, t, 1:2], st1[:, t, 0:1], 1, D, S["rstd_ok"])

                @block.scalar
                def _(act):
                    for b in range(NB):
                        act.wait_ge(S["bc_mm"], DC // 4 * (b + 1))
                        dst = gA[:, b] if b < 2 else gB[:, b - 2]
                        nc.scalar.activation(dst.rearrange("p (b n) -> p b n", b=2), bank[:, 0:2, :], ACT.Copy
                                             ).then_inc(S["bc_ok"], 1)

                    def oT_out(t):
                        act.wait_ge(S["oT_mm"], t + 1)
                        if t >= 2:
                            act.wait_ge(S["mm_done"], t - 1)
                        nc.scalar.activation(oTh[:, t % 2].rearrange("p (b c) n -> p b (c n)", b=2), bank[:, 2:4, :], ACT.Copy,
                                             scale=sub8[:]).then_inc(S["oT_ok"], 1)

                    if attn:
                        oT_out(0)
                        for i in range(H):
                            act.wait_ge(wo_in[i], 16)
                            nc.scalar.activation(woh[:, i], woraw[raw_of(i)], ACT.Copy).then_inc(S["wo_hi"], 1)
                    for s in range(TT + 2):
                        if attn and s + 1 < TT:
                            oT_out(s + 1)
                        if s < TT:
                            act.wait_ge(S["x_ok"], s + 1)
                            if s >= 2:
                                act.wait_ge(xn_out[s % 2], 16 * (s // 2))
                                act.wait_ge(S["xT_mm"], s - 1)
                            nc.scalar.activation(xn[:, s % 2], xt[:, s % 2], ACT.Square, accum_out=st1[:, s, 0:1]
                                                 ).then_inc(S["ssq_ok"], 1)
                            act.wait_ge(S["ssq_ok"], s + 1)
                            act.wait_ge(S["rstd_ok"], s + 1)
                            nc.scalar.activation(xn[:, s % 2], xt[:, s % 2], ACT.Copy, scale=st1[:, s, 1:2]
                                                 ).then_inc(S["xn_ok"], 1)
                        if s >= 2:
                            t = s - 2
                            act.wait_ge(S["lmax_ok"], t + 1)
                            nc.scalar.activation(sm[:, t % 2, 0], bank[:, 6, 0:E], ACT.Exp, bias=st1[:, t, 2:3],
                                                 accum_out=st1[:, t, 3:4]).then_inc(S["lexp_ok"], 1)

                @block.vector
                def _(dve):
                    step = Step(dve, S["dve_step"])
                    step.count(nc.vector.memset(ap[:], 0.0))
                    step.count(nc.vector.memset(af[:], 0.0))
                    for cond in range(2):
                        step.count(nc.vector.scalar_tensor_tensor(
                            gains[:, g2, :, cond], modc[:, base + SCALE2 * DC:base + SCALE2 * DC + DC, cond], 1.0,
                            colsA[:, 112 + layer * DC:112 + layer * DC + DC], ALU.add, ALU.mult))
                    if not attn:
                        for cond in range(2):
                            gate = modc[:, base + GATE1 * DC:base + GATE1 * DC + DC, cond]
                            step.link(nc.vector.tensor_tensor(pcol[:, 0, :, cond], gate, colsB[:, 24:32], ALU.mult))
                            step.link(nc.vector.tensor_tensor(pcol[:, 1, :, cond], pcol[:, 0, :, cond], colsB[:, 16:24], ALU.mult))
                    n = 0
                    for b in range(NB):
                        for c in range(0, DC, 4):
                            if n >= 2:
                                dve.wait_ge(S["bc_mm"], n - 1)
                            col = (modc[:, base + GATE1 * DC + c:base + GATE1 * DC + c + 4, b] if attn
                                   else pcol[:, b // 2, c:c + 4, b % 2])
                            nc.vector.tensor_tensor(dg[:, n % 2], ident[:].unsqueeze(1).to_broadcast([P, 4, P]),
                                                    col.unsqueeze(2).to_broadcast([P, 4, P]), ALU.mult).then_inc(S["dg_ok"], 1)
                            n += 1

                    def head_norm(t):
                        if t:
                            dve.wait_ge(S["oT_mm"], t)
                        dve.wait_ge(o_in[t % 2], 16 * (t // 2) + 16)
                        o = oin[:, t % 2].rearrange("p (h d) -> p h d", h=H)
                        m = om[:].rearrange("p (h d) -> p h d", h=H)
                        step.link(nc.vector.tensor_tensor(om[:], oin[:, t % 2], oin[:, t % 2], ALU.mult))
                        nc.vector.tensor_reduce(osm[:, t % 2, 0], m, AX.X, ALU.add).then_inc(S["oss_ok"], 1)
                        dve.wait_ge(S["orstd_ok"], t + 1)
                        dve.wait_ge(S["oss_ok"], t + 1)
                        nc.vector.tensor_tensor(m, o, osm[:, t % 2, 1].unsqueeze(2).to_broadcast([P, H, VD]), ALU.mult
                                                ).then_inc(S["om_ok"], 1)

                    def oT_low(t):
                        dve.wait_ge(S["oT_ok"], t + 1)
                        nc.vector.scalar_tensor_tensor(oTl[:, t % 2].rearrange("p (b c) n -> p b (c n)", b=2), bank[:, 2:4, :],
                                                       sub8[:], oTh[:, t % 2].rearrange("p (b c) n -> p b (c n)", b=2).bitcast(F32),
                                                       ALU.mult, ALU.subtract).then_inc(S["oTl_ok"], 1)

                    if attn:
                        head_norm(0)
                        oT_low(0)
                        for i in range(H):
                            dve.wait_ge(S["wo_hi"], i + 1)
                            nc.vector.tensor_tensor(wol[:, i], woraw[raw_of(i)], woh[:, i].bitcast(F32), ALU.subtract
                                                    ).then_inc(S["wo_lo"], 1)
                    for s in range(TT + 3):
                        if attn and s + 1 < TT:
                            head_norm(s + 1)
                        if s < TT:
                            cond = cond_of[s]
                            dve.wait_ge(S["mm_done"], s + 1)
                            dve.wait_ge(S["bc_ok"], NB)
                            dve.wait_ge(x_in_s[s % 2], 16 * (s // 2 + 1))
                            y = bank[:, PB[s % 2]:PB[s % 2] + 2, :]
                            nc.vector.tensor_tensor(y, y, gA[:, cond].rearrange("p (b n) -> p b n", b=2), ALU.mult
                                                    ).then_inc(S["xu"], 1)
                            if not attn:
                                dve.wait_ge(S["xb_ok"], s + 1)
                            dve.wait_ge(S["xu"], s + 1)
                            xv = xt[:, s % 2].rearrange("p (b n) -> p b n", b=2)
                            nc.vector.tensor_tensor(xv, xv, y, ALU.add).then_inc(S["x_ok"], 1)
                            dve.wait_ge(S["x_ok"], s + 1)
                            nc.vector.memset(st1[:, s, 4:5], 0.0).then_inc(S["tmp_ok"], 1)
                            if attn and s + 1 < TT:
                                oT_low(s + 1)
                        if 1 <= s <= TT:
                            t = s - 1
                            dve.wait_ge(S["xT_mm"], t + 1)
                            if t >= 2:
                                dve.wait_ge(S["lg_mm"], t - 1)
                            cond = cond_of[t]
                            dve.wait_ge(S["dve_step"], 4)
                            for c in range(DC):
                                last = nc.vector.tensor_scalar(
                                    h2[:, t % 2, c], bank[:, 4 + c // 4, (c % 4) * P:(c % 4 + 1) * P],
                                    gains[:, g2, c, cond:cond + 1], modc[:, base + SHIFT2 * DC + c, cond:cond + 1],
                                    ALU.mult, ALU.add)
                            last.then_inc(S["h2_ok"], 1)
                        if 2 <= s <= TT + 1:
                            t = s - 2
                            dve.wait_ge(S["lg_mm"], t + 1)
                            nc.vector.tensor_reduce(st1[:, t, 2:3], bank[:, 6, 0:E], AX.X, ALU.max, negate=True
                                                    ).then_inc(S["lmax_ok"], 1)
                            dve.wait_ge(S["lexp_ok"], t + 1)
                            step.link(nc.vector.reciprocal(st1[:, t, 5:6], st1[:, t, 3:4]))
                            if t >= 2:
                                dve.wait_ge(S["affT_mm"], t - 1)
                            lo = HI if LT // 2 <= t < LT else 0
                            nc.vector.tensor_scalar(ap[:, t % 2, lo:lo + E], sm[:, t % 2, 0], st1[:, t, 5:6], None, ALU.mult
                                                    ).then_inc(S["aff_ok"], 1)
                        if s >= 3:
                            t = s - 3
                            dve.wait_ge(S["affT_mm"], t + 1)
                            lo = HI if LT // 2 <= t < LT else 0
                            c0 = HALF if t == LT else (t % (LT // 2)) * P
                            nc.vector.tensor_copy(af[lo:lo + E, c0:c0 + P], bank[lo:lo + E, 7, 0:P]).then_inc(S["af_ok"], 1)
                    dve.wait_ge(S["af_ok"], TT)
                    for vals, idx, rows_, lo, n, cap in ((vv, ii, HI + E, 0, HALF, CAP_L), (vc, ic, E, HALF, N_CTX, CAP_C)):
                        work = af[0:rows_, lo:lo + n]
                        for r in range(cap // 8):
                            v8 = vals[0:rows_, 8 * r:8 * r + 8]
                            step.link(nc.vector.max(v8, work))
                            step.link(nc.vector.max_index(idx[0:rows_, 8 * r:8 * r + 8], v8, work))
                            step.link(nc.vector.match_replace(work, v8, work, -1.0))
                    step.link(nc.vector.tensor_copy(fi[0:HI + E], ii[0:HI + E]))
                    nc.vector.tensor_copy(fc[0:E], ic[0:E]).then_inc(S["top_lists"], 1)
                    dve.wait_ge(S["top_mm"], 1)
                    step.count(nc.vector.tensor_copy(valC[0:CAP_C, 0:E], bank[0:CAP_C, 0, 128:128 + E]))
                    step.count(nc.vector.tensor_copy(idxC[0:CAP_C, 0:E], bank[0:CAP_C, 0, 160:160 + E]))
                    nc.vector.tensor_copy(rb[:].rearrange("p (k e) -> p k e", k=2),
                                          bank[:, 0, 0:128].rearrange("p (k e) -> p k e", k=2)[:, :, HI:HI + E]
                                          ).then_inc(S["top_lists"], 1)
                    dve.wait_ge(S["top_mm"], 2)
                    vA, vB = bank[:, 0, 0:E], bank[:, 1, 0:E]
                    iA, iB = bank[:, 0, 64:64 + E], bank[:, 1, E:2 * E]
                    step.count(nc.vector.tensor_copy(mk[:, 0], vB))
                    step.link(nc.vector.tensor_copy(mk[:, 1], iB))
                    step.count(nc.vector.tensor_tensor(valL[:, 0:E], vA, mk[:, 0], ALU.max))
                    step.count(nc.vector.tensor_tensor(mk[:, 2], vA, mk[:, 0], ALU.is_ge))
                    step.link(nc.vector.tensor_tensor(rb[:, 0:E], iA, mk[:, 1], ALU.subtract))
                    step.link(nc.vector.scalar_tensor_tensor(rb[:, E:2 * E], rb[:, 0:E], -float(HALF), mk[:, 2], ALU.add, ALU.mult))
                    step.link(nc.vector.scalar_tensor_tensor(idxL[:, 0:E], mk[:, 1], float(HALF), rb[:, E:2 * E], ALU.add, ALU.add))
                    for x, parts in ((valL, P), (idxL, P), (valC, CAP_C), (idxC, CAP_C)):
                        nc.vector.tensor_copy(x[0:parts, E:E + 1], x[0:parts, 0:1])

        def experts(layer):
            g2 = 2 * layer + 1
            base = layer * SECT
            with Stage() as st:
                off = exp_at
                xe, off = sb(f"ex_xe{layer}", [P, D], off)
                xeC, off = sb(f"ex_xeC{layer}", [P, D], off)
                xT, off = sb(f"ex_xT{layer}", [P, DC, CAP], off)
                hid, off = sb(f"ex_hid{layer}", [P, FF // P, CAP], off)
                ge, off = sb(f"ex_ge{layer}", [P, 2, 3 * CAP], off)
                t1, off = sb(f"ex_t1{layer}", [P, 3 * CAP], off)
                t2, off = sb(f"ex_t2{layer}", [P, 3 * CAP], off)
                yT, off = sb(f"ex_yT{layer}", [P, DC, CAP], off)
                ye, off = sb(f"ex_ye{layer}", [P, D], off)
                yeC, off = sb(f"ex_yeC{layer}", [P, D], off)
                gi, off = sb(f"ex_gi{layer}", [P, 2], off, U32)
                si, off = sb(f"ex_si{layer}", [P, 2], off, U32)
                assert off <= nc.sbuf_usable_end, off
                S = {}
                for n in ("xe_in xeT_mm xT_ok gate_mm up_mm exp_ok hid_step hid_ok y_mm yT_ok yT_mm ye_ok yeC_ok ye_read yeC_read ye_free gidx0_ok gidx_ok "
                          "sidx_ok").split():
                    S[n] = sem(st, f"ex{layer}_" + n)
                scat = sem(st, f"ex{layer}_scattered")
                block = st.enter_context(nc.Block())
                NJ = len(PIECES)
                r0 = 16 * E * layer
                GB, UB, YB, TB = (0, 1), (2, 3), (4, 5, 6), 7

                @block.sync
                def _(sp):
                    sp.wait_ge(S["xe_in"], 32)
                    for i in range(RING_EARLY[layer], 12):
                        dst, src = ring_source(layer, 0, i)
                        sp.dma_start(dst, src).then_inc(ring_in[i], 16)
                    with sp.Fori(1, E) as e:
                        for j in range(NJ):
                            sp.wait_ge(S["up_mm"], NJ * e - NJ + j + 1)
                            for i in (2 * j, 2 * j + 1):
                                dst, src = ring_source(layer, e, i)
                                sp.dma_start(dst, src).then_inc(ring_in[i], 16)
                        sp.wait_ge(S["y_mm"], 3 * e + 1)
                        for i in range(8, 12):
                            dst, src = ring_source(layer, e, i)
                            sp.dma_start(dst, src).then_inc(ring_in[i], 16)

                @block.gpsimd
                def _(pool):
                    def gather(e, copied, count):
                        nc.gpsimd.tensor_copy(gi[:, 0:1], idxL[:, bass.ds(e, 1)])
                        nc.gpsimd.tensor_copy(gi[0:CAP_C, 1:2], idxC[0:CAP_C, bass.ds(e, 1)]).then_inc(copied, 1)
                        pool.wait_ge(S["gidx0_ok"], 1)
                        pool.wait_ge(copied, count)
                        nc.gpsimd.indirect_dma_start(out=xe[:], out_offset=None, in_=xnrm[0],
                                                     in_offset=bass.IndirectOffsetOnAxis(ap=gi[:, 0:1], axis=0)
                                                     ).then_inc(S["xe_in"], 16)
                        nc.gpsimd.indirect_dma_start(out=xeC[0:CAP_C], out_offset=None, in_=xnrm[1],
                                                     in_offset=bass.IndirectOffsetOnAxis(ap=gi[0:CAP_C, 1:2], axis=0)
                                                     ).then_inc(S["xe_in"], 16)

                    for n in ("ye_free", "ye_read", "yeC_read"):
                        pool.sem_inc(S[n], 1)
                    gather(0, S["gidx0_ok"], 1)
                    with pool.Fori(0, E) as e:
                        pool.wait_ge(S["xeT_mm"], 3 * e + 3)
                        pool.wait_ge(S["xe_in"], 32 * e + 32)
                        gather(e + 1, S["gidx_ok"], e + 1)
                        nc.gpsimd.tensor_copy(si[:, 0:1], idxL[:, bass.ds(e, 1)])
                        nc.gpsimd.tensor_copy(si[0:CAP_C, 1:2], idxC[0:CAP_C, bass.ds(e, 1)]).then_inc(S["sidx_ok"], 1)
                        pool.wait_ge(S["ye_ok"], 1)
                        pool.wait_ge(S["sidx_ok"], e + 1)
                        pool.wait_ge(S["ye_ok"], e + 1)
                        nc.gpsimd.indirect_dma_start(out=xres[0], out_offset=bass.IndirectOffsetOnAxis(ap=si[:, 0:1], axis=0),
                                                     in_=ye[:], in_offset=None, compute_op=ALU.add).then_inc(scat, 16)
                        pool.sem_inc(S["ye_read"], 1)
                        pool.wait_ge(S["yeC_ok"], 1)
                        pool.wait_ge(S["yeC_ok"], e + 1)
                        nc.gpsimd.indirect_dma_start(out=xres[1], out_offset=bass.IndirectOffsetOnAxis(ap=si[0:CAP_C, 1:2], axis=0),
                                                     in_=yeC[0:CAP_C], in_offset=None, compute_op=ALU.add).then_inc(scat, 16)
                        pool.sem_inc(S["yeC_read"], 1)
                        pool.wait_ge(scat, 32 * e + 32)
                        pool.sem_inc(S["ye_free"], 1)
                    pool.wait_ge(S["xe_in"], 32 * E + 32)
                    pool.wait_ge(scat, 32 * E)

                @block.tensor
                def _(pe):
                    def turn_x(n, first=False):
                        pe.wait_ge(S["xe_in"], 32 * n + 32)
                        if not first:
                            pe.wait_ge(S["yeC_read"], n)
                        for b, c0 in ((YB[2], 0), (TB, 4)):
                            for c in range(c0, c0 + 4):
                                last = nc.tensor.transpose(bank[:, b, (c - c0) * P:(c - c0 + 1) * P], xe[:, c * P:(c + 1) * P], ident[:])
                            last.then_inc(S["xeT_mm"], 1)
                        for c in range(DC):
                            last = nc.tensor.transpose(bank[:, YB[1], c * CAP_C:(c + 1) * CAP_C], xeC[0:CAP_C, c * P:(c + 1) * P],
                                                       ident[0:CAP_C, 0:CAP_C])
                        last.then_inc(S["xeT_mm"], 1)

                    pe.sem_inc(S["y_mm"], 1)
                    pe.sem_inc(S["yT_mm"], 1)
                    turn_x(0, first=True)
                    with pe.Fori(0, E) as e:
                        pe.wait_ge(S["xT_ok"], 3 * e + 3)
                        for j, nf in enumerate(PIECES):
                            pe.wait_ge(S["hid_ok"], NJ * e + j + 1)
                            if j == 1:
                                pe.wait_ge(S["ye_read"], e + 1)
                            for banks, i, done in ((GB, 2 * j, "gate_mm"), (UB, 2 * j + 1, "up_mm")):
                                pe.wait_ge(ring_in[i], r0 + 16 * e + 16)
                                wv = ring[i][:, 0:DC * nf * P].rearrange("p (c f) -> p c f", c=DC)
                                for f in range(nf):
                                    for c in range(DC):
                                        last = nc.tensor.matmul(bank[:, banks[j % 2], f * CAP:(f + 1) * CAP],
                                                                wv[:, c, f * P:(f + 1) * P], xT[:, c],
                                                                start=(c == 0), stop=(c == DC - 1))
                                last.then_inc(S[done], 1)
                        turn_x(e + 1)
                        for m in range(DC):
                            if m == 3:
                                pe.wait_ge(S["xT_ok"], 3 * e + 6)
                            f = 0
                            for j, nf in enumerate(PIECES):
                                if m == 0:
                                    pe.wait_ge(S["hid_ok"], NJ * e + j + 3)
                                    pe.wait_ge(ring_in[8 + j], r0 + 16 * e + 16)
                                wv = ring[8 + j][:, 0:nf * D].rearrange("p (q d) -> p q d", q=nf)
                                for q in range(nf):
                                    last = nc.tensor.matmul(bank[:, YB[m // 3], (m % 3) * CAP:(m % 3 + 1) * CAP],
                                                            wv[:, q, m * P:(m + 1) * P], hid[:, f],
                                                            start=(f == 0), stop=(f == FF // P - 1))
                                    f += 1
                            if m in (2, 5, 7):
                                last.then_inc(S["y_mm"], 1)
                        for m in range(DC):
                            pe.wait_ge(S["yT_ok"], DC * e + m + 1)
                            last = nc.tensor.transpose(bank[:, (GB[1], UB[1])[m // 4], (m % 4) * P:(m % 4 + 1) * P],
                                                       yT[:, m, 0:P], ident[:])
                        last.then_inc(S["yT_mm"], 1)
                        for m in range(DC):
                            last = nc.tensor.transpose(bank[0:CAP_C, (TB, YB[0])[m // 4], (m % 4) * P:(m % 4 + 1) * P],
                                                       yT[:, m, P:CAP], ident[:])
                        last.then_inc(S["yT_mm"], 1)

                @block.scalar
                def _(act):
                    with act.Fori(0, E) as e:
                        for j, nf in enumerate(PIECES):
                            act.wait_ge(S["gate_mm"], NJ * e + j + 1)
                            act.wait_ge(S["hid_ok"], NJ * e + j + 1)
                            nc.scalar.activation(ge[:, j % 2, 0:nf * CAP], bank[:, GB[j % 2], 0:nf * CAP], ACT.Exp, scale=-1.0
                                                 ).then_inc(S["exp_ok"], 1)
                        act.wait_ge(S["yT_mm"], 2 * e + 1)
                        for m in range(DC):
                            if m % 3 == 0:
                                act.wait_ge(S["y_mm"], 3 * e + m // 3 + 2)
                            src = bank[:, YB[m // 3], (m % 3) * CAP:(m % 3 + 1) * CAP]
                            gate = modc[:, base + GATE2 * DC + m]
                            nc.scalar.activation(yT[:, m, 0:P], src[:, 0:P], ACT.Copy, scale=gate[:, 0:1])
                            nc.scalar.activation(yT[:, m, P:CAP], src[:, P:CAP], ACT.Copy, scale=gate[:, 1:2]
                                                 ).then_inc(S["yT_ok"], 1)
                        act.wait_ge(S["yT_mm"], 2 * e + 2)
                        act.wait_ge(S["ye_free"], e + 1)
                        for i, b in enumerate((GB[1], UB[1])):
                            last = nc.scalar.activation(ye[:, i * 512:(i + 1) * 512], bank[:, b], ACT.Copy,
                                                        scale=valL[:, bass.ds(e, 1)])
                        last.then_inc(S["ye_ok"], 1)

                @block.vector
                def _(dve):
                    nc.vector.memset(t1[:, 0:8], 0.0).then_inc(S["hid_ok"], 1)
                    nc.vector.memset(t2[:, 0:8], 0.0).then_inc(S["hid_ok"], 1)
                    dve.wait_ge(S["hid_ok"], 2)

                    def adaln(n):
                        for b, c0 in ((YB[2], 0), (TB, 4)):
                            dve.wait_ge(S["xeT_mm"], 3 * n + 1 + c0 // 4)
                            for c in range(c0, c0 + 4):
                                last = nc.vector.tensor_scalar(xT[:, c, 0:P], bank[:, b, (c - c0) * P:(c - c0 + 1) * P],
                                                               gains[:, g2, c, 0:1], modc[:, base + SHIFT2 * DC + c, 0:1],
                                                               ALU.mult, ALU.add)
                            last.then_inc(S["xT_ok"], 1)
                        dve.wait_ge(S["xeT_mm"], 3 * n + 3)
                        for c in range(DC):
                            last = nc.vector.tensor_scalar(xT[:, c, P:CAP], bank[:, YB[1], c * CAP_C:(c + 1) * CAP_C],
                                                           gains[:, g2, c, 1:2], modc[:, base + SHIFT2 * DC + c, 1:2],
                                                           ALU.mult, ALU.add)
                        last.then_inc(S["xT_ok"], 1)

                    adaln(0)
                    with dve.Fori(0, E) as e:
                        for j, nf in enumerate(PIECES):
                            n = nf * CAP
                            step = Step(dve, S["hid_step"], 3 * NJ * e + 3 * j)
                            dve.wait_ge(S["exp_ok"], NJ * e + j + 1)
                            dve.wait_ge(S["hid_ok"], NJ * e + j + 2)
                            step.link(nc.vector.tensor_scalar(t1[:, 0:n], ge[:, j % 2, 0:n], 1.0, None, ALU.add))
                            step.link(nc.vector.reciprocal(t2[:, 0:n], t1[:, 0:n]))
                            step.link(nc.vector.tensor_tensor(t1[:, 0:n], bank[:, GB[j % 2], 0:n], t2[:, 0:n], ALU.mult))
                            dve.wait_ge(S["up_mm"], NJ * e + j + 1)
                            if j == 0:
                                dve.wait_ge(S["y_mm"], 3 * e + 1)
                            nc.vector.tensor_tensor(hid[:, PIECE0[j]:PIECE0[j] + nf].rearrange("p f s -> p (f s)"), t1[:, 0:n],
                                                    bank[:, UB[j % 2], 0:n], ALU.mult).then_inc(S["hid_ok"], 1)
                        adaln(e + 1)
                        dve.wait_ge(S["yT_mm"], 2 * e + 3)
                        dve.wait_ge(S["ye_free"], e + 1)
                        for i, b in enumerate((TB, YB[0])):
                            last = nc.vector.tensor_scalar(yeC[0:CAP_C, i * 512:(i + 1) * 512], bank[0:CAP_C, b],
                                                           valC[0:CAP_C, bass.ds(e, 1)], None, ALU.mult)
                        last.then_inc(S["yeC_ok"], 1)

        PAD = 8
        WL = N_LAT + 2 * PAD
        WIDE = WL + N_CTX + 2 * PAD

        def pool_mixer(hw, off):
            with Stage() as st:
                xt, off = sb("pm_xt", [P, 4, D], off)
                s1, off = sb("pm_s1", [P, 2, WIDE], off)
                s2, off = sb("pm_s2", [P, 2, WIDE], off)
                edge, off = sb("pm_edge", [P, len(WINDOWS), 2, 2, EDGE], off)
                sq, off = sb("pm_sq", [P, D], off)
                st1, off = sb("pm_st", [P, TT, 2], off)
                assert off <= nc.sbuf_usable_end, off
                S = {}
                for n in "edge_in ssq_ok rstd_ok xn_ok xT_mm h_ok step pool_step win_step zero_ok".split():
                    S[n] = sem(st, "pm_" + n)
                x_s = [sem(st, f"pm_x_in{i}") for i in range(4)]
                block = st.enter_context(nc.Block())

                def place_of(t):
                    return PAD + t * P if t < LT else WL + PAD

                POOL_CHUNKS = 3

                def windows(eng, ops, step, scratch, c):
                    if c in (0, POOL_CHUNKS):
                        eng.wait_ge(S["h_ok"], TT)
                        eng.wait_ge(S["zero_ok"], 5)
                        eng.wait_ge(S["edge_in"], 16)
                    g = c * P // GROUP
                    src = hw[:, c]
                    back, fwd = 1, 0
                    for k in range(g + 1):
                        dst = scratch[:, k % 2]
                        lo, hi = back, WIDE - fwd
                        step.link(ops.tensor_tensor(dst[:, lo:hi], src[:, lo - back:hi - back], src[:, lo + fwd:hi + fwd], ALU.add))
                        src, back, fwd = dst, WINDOWS[k] // 2, WINDOWS[k] // 2
                    for i, (p0, n) in enumerate(((PAD, N_LAT), (WL + PAD, N_CTX))):
                        for j, at in enumerate((p0, p0 + n - EDGE)):
                            step.count(ops.tensor_tensor(src[:, at:at + EDGE], src[:, at:at + EDGE], edge[:, g, i, j], ALU.mult))
                    step.wait()
                    mid = slice(PAD, WIDE - PAD)
                    if ops is nc.vector:
                        step.link(ops.scalar_tensor_tensor(hw[:, c, mid], src[:, mid], 1.0 / WINDOWS[g], hw[:, c, mid],
                                                           ALU.mult, ALU.subtract))
                    else:
                        step.link(ops.tensor_scalar(src[:, mid], src[:, mid], 1.0 / WINDOWS[g], None, ALU.mult))
                        step.link(ops.tensor_tensor(hw[:, c, mid], src[:, mid], hw[:, c, mid], ALU.subtract))

                @block.sync
                def _(sp):
                    for t in range(TT):
                        if t >= 4:
                            sp.wait_ge(S["xT_mm"], t - 3)
                        sp.dma_start(xt[:, t % 4], rows(xres, t)).then_inc(x_s[t % 4], 16)
                        if t == 3:
                            sp.dma_start(edge[:].rearrange("p g i j n -> p (g i j n)"),
                                         a["window_edge"].rearrange("g i j n -> (g i j n)").partition_broadcast(P)
                                         ).then_inc(S["edge_in"], 16)

                @block.gpsimd
                def _(pool):
                    for i, (lo, n) in enumerate(((0, PAD), (PAD + N_LAT, 2 * PAD), (WIDE - PAD, PAD))):
                        nc.gpsimd.memset(hw[:, :, lo:lo + n], 0.0).then_inc(S["zero_ok"], 1)
                    for x in (s1, s2):
                        nc.gpsimd.memset(x[:], 0.0).then_inc(S["zero_ok"], 1)
                    for t in range(TT):
                        pool.wait_ge(S["ssq_ok"], t + 1)
                        nc.gpsimd.tensor_scalar(st1[:, t, 0:1], st1[:, t, 0:1], 1.0 / D, EPS, ALU.mult, ALU.add
                                                ).then_inc(S["pool_step"], 1)
                        pool.wait_ge(S["pool_step"], t + 1)
                        nc.gpsimd.tensor_tensor(st1[:, t, 1:2], st1[:, t, 0:1], hpow[:, 0:1], ALU.pow).then_inc(S["rstd_ok"], 1)
                    win = Step(pool, S["win_step"])
                    for c in range(POOL_CHUNKS):
                        windows(pool, nc.gpsimd, win, s2, c)

                @block.scalar
                def _(act):
                    for t in range(TT):
                        act.wait_ge(x_s[t % 4], 16 * (t // 4 + 1))
                        if t:
                            act.wait_ge(S["ssq_ok"], t)
                        nc.scalar.activation(sq[:], xt[:, t % 4], ACT.Square, accum_out=st1[:, t, 0:1]).then_inc(S["ssq_ok"], 1)
                        act.wait_ge(S["rstd_ok"], t + 1)
                        nc.scalar.activation(xt[:, t % 4], xt[:, t % 4], ACT.Copy, scale=st1[:, t, 1:2]).then_inc(S["xn_ok"], 1)

                @block.tensor
                def _(pe):
                    for t in range(TT):
                        pe.wait_ge(S["xn_ok"], t + 1)
                        if t >= 4:
                            pe.wait_ge(S["h_ok"], t - 3)
                        for c in range(DC):
                            last = nc.tensor.transpose(bank[:, 2 * (t % 4) + c // 4, (c % 4) * P:(c % 4 + 1) * P],
                                                       xt[:, t % 4, c * P:(c + 1) * P], ident[:])
                        last.then_inc(S["xT_mm"], 1)

                @block.vector
                def _(dve):
                    step = Step(dve, S["step"])
                    for cond in range(2):
                        last = nc.vector.scalar_tensor_tensor(gains[:, 2, :, cond], modc[:, SECT + SCALE1 * DC:SECT + SCALE1 * DC + DC, cond],
                                                              1.0, colsA[:, 96 + DC:96 + 2 * DC], ALU.add, ALU.mult)
                    step.link(last)
                    for t in range(TT):
                        dve.wait_ge(S["xT_mm"], t + 1)
                        cond = 0 if t < LT else 1
                        for c in range(DC):
                            last = nc.vector.tensor_scalar(hw[:, c, place_of(t):place_of(t) + P],
                                                           bank[:, 2 * (t % 4) + c // 4, (c % 4) * P:(c % 4 + 1) * P],
                                                           gains[:, 2, c, cond:cond + 1],
                                                           modc[:, SECT + SHIFT1 * DC + c, cond:cond + 1], ALU.mult, ALU.add)
                        last.then_inc(S["h_ok"], 1)
                    for c in range(POOL_CHUNKS, DC):
                        windows(dve, nc.vector, step, s1, c)

        def final_norm():
            off = persistent_end
            with Stage() as st:
                xt, off = sb("fn_xt", [P, TT, D], off)
                yt, off = sb("fn_yt", [P, TT, D], off)
                fg, off = sb("fn_fg", [P, D], off)
                sq, off = sb("fn_sq", [P, D], off)
                st1, off = sb("fn_st", [P, TT, 2], off)
                S = {n: sem(st, "fn_" + n) for n in "fg_in ssq_ok rstd_ok y_ok out_ok pool_step".split()}
                x_s = [sem(st, f"fn_x_in{t}") for t in range(TT)]
                block = st.enter_context(nc.Block())
                y_out = [out["y_sample"][0], out["y_prompt"][0]]

                @block.sync
                def _(sp):
                    for t in range(TT):
                        sp.dma_start(xt[:, t], rows(xres, t)).then_inc(x_s[t], 16)
                        if t == 0:
                            sp.dma_start(fg[:], a["final_g"].partition_broadcast(P)).then_inc(S["fg_in"], 16)
                    for t in range(TT):
                        sp.wait_ge(S["y_ok"], t + 1)
                        sp.dma_start(rows(y_out, t), yt[:, t]).then_inc(S["out_ok"], 16)
                    sp.wait_ge(S["out_ok"], 16 * TT)

                @block.scalar
                def _(act):
                    for t in range(TT):
                        act.wait_ge(x_s[t], 16)
                        if t:
                            act.wait_ge(S["ssq_ok"], t)
                        nc.scalar.activation(sq[:], xt[:, t], ACT.Square, accum_out=st1[:, t, 0:1]).then_inc(S["ssq_ok"], 1)

                @block.gpsimd
                def _(pool):
                    for t in range(TT):
                        pool.wait_ge(S["ssq_ok"], t + 1)
                        nc.gpsimd.tensor_scalar(st1[:, t, 0:1], st1[:, t, 0:1], 1.0 / D, EPS, ALU.mult, ALU.add
                                                ).then_inc(S["pool_step"], 1)
                        pool.wait_ge(S["pool_step"], t + 1)
                        nc.gpsimd.tensor_tensor(st1[:, t, 1:2], st1[:, t, 0:1], hpow[:, 0:1], ALU.pow).then_inc(S["rstd_ok"], 1)

                @block.vector
                def _(dve):
                    dve.wait_ge(S["fg_in"], 16)
                    for t in range(TT):
                        dve.wait_ge(S["rstd_ok"], t + 1)
                        nc.vector.scalar_tensor_tensor(yt[:, t], xt[:, t], st1[:, t, 1:2], fg[:], ALU.mult, ALU.mult
                                                       ).then_inc(S["y_ok"], 1)

        hTh = nc.alloc_sbuf_tensor_at("hTh", [P, DC, N_TOK], F32R, offset=persistent_end)
        hTl = nc.alloc_sbuf_tensor_at("hTl", [P, DC, N_TOK], F32R, offset=persistent_end + 4 * DC * N_TOK)
        setup_and_norm(hTh, hTl)
        attention(hTh, hTl, persistent_end + 2 * 4 * DC * N_TOK)
        mixer_and_route(0, None, ring_at + RING_EARLY[0] * SB)
        experts(0)
        hw = nc.alloc_sbuf_tensor_at("hw", [P, DC, WIDE], F32, offset=big_at)
        pool_mixer(hw, ring_at)
        class Tiles:
            def __getitem__(self, key):
                _, c, t = key
                p0 = PAD + t * P if t < LT else WL + PAD
                return hw[:, c, p0:p0 + P]
        mixer_and_route(1, Tiles(), late_at)
        experts(1)
        final_norm()


_INS = ['x_prompt', 'x_sample', 'cache_k', 'cache_v', 'c', 'c_ctx', 'w_mod', 'b_mod', 'norm1_g', 'norm2_g',
        'attn_wqkv', 'attn_wo', 'lambda_q1', 'lambda_k1', 'lambda_q2', 'lambda_k2', 'subln_g', 'pool_w', 'pool_b',
        'pool_scale', 'router_w', 'expert_w_gate', 'expert_w_up', 'expert_w_down', 'final_g']
_OUTS = [('y_prompt', (1, 128, 1024)), ('y_sample', (1, 1024, 1024)), ('new_cache_k', (1, 1, 128, 8, 128)),
         ('new_cache_v', (1, 1, 128, 8, 128))]


def kernel(**inputs):
    import concourse.bacc as _bacc
    from concourse.bass_utils import run_bass_kernel_spmd as _run

    nc = _bacc.Bacc("TRN2", target_bir_lowering=False, num_devices=1)
    arrays, a, out = {}, {}, {}
    cos, sin = rope_tables()
    eye = np.eye(P, dtype=np.float32)
    constants = {"rope_cos": cos, "rope_sin": sin, "window_edge": window_edges(), "ident": eye, "anti": eye[::-1]}
    for name, x in [*((n, inputs[n]) for n in _INS), *constants.items()]:
        x = np.ascontiguousarray(x)
        arrays[f"in_{name}"] = x
        a[name] = nc.dram_tensor(f"in_{name}", x.shape, mybir.dt.from_np(x.dtype), kind="ExternalInput").ap()
    for name, shape in _OUTS:
        out[name] = nc.dram_tensor(f"out_{name}", shape, F32, kind="ExternalOutput").ap()
    build(nc, a, out)
    r = _run(nc, [arrays], core_ids=[0])
    return tuple(r.results[0][f"out_{name}"] for name, _ in _OUTS)
```
